# Optimizing a Trainium2 kernel written in Bass

```python
import math
import jax, jax.numpy as jnp
from jax import lax
import numpy as np

D_MODEL = 1024
BATCH = 1
SEQ = 512
DEPTH = 1
DEC_BATCH = 8
DEC_SEQ = 8
PAST_LEN = 4096
PAGE_SIZE = 128

D_MIX = D_MODEL
GLA_WIDTH = D_MIX // 2
GLA_HEADS = 4
GLA_DK = GLA_WIDTH // 2 // GLA_HEADS
GLA_DV = GLA_WIDTH // GLA_HEADS
GLA_RANK = 16
GLA_TAU = 16.0
GLA_CHUNK = 64
GMLP_WIDTH = D_MIX - GLA_WIDTH
GMLP_HEADS = 4
GMLP_DH = GMLP_WIDTH // GMLP_HEADS
GMLP_CHUNK = 128
QK_WIDTH = GLA_HEADS * GLA_DK
N_IN = 2 * QK_WIDTH + 2 * GLA_WIDTH + GLA_RANK + 2 * GMLP_WIDTH
N_EXPERTS = 64
TOP_K = 8
N_GROUPS = 8
TOPK_GROUPS = 4
D_EXPERT = 256
D_SHARED = 256
ROUTE_SCALE = 2.5
ALPHA = (2.0 * DEPTH) ** 0.25
BETA = (8.0 * DEPTH) ** -0.25

kernel_name = 'hymba_gla_gmlp_moe_deepnorm_step'

def layernorm(x, g, b, eps=1e-5):
    xf = x.astype(jnp.float32)
    mu = xf.mean(-1, keepdims=True)
    var = jnp.square(xf - mu).mean(-1, keepdims=True)
    return ((xf - mu) * lax.rsqrt(var + eps) * g + b).astype(x.dtype)

def head_rmsnorm(x, g, eps=1e-6):
    xf = x.astype(jnp.float32)
    return xf * lax.rsqrt(jnp.square(xf).mean(-1, keepdims=True) + eps) * g

def gla_scan(q, k, v, log_a, s0):
    B, T, H, DK = q.shape
    DV = v.shape[-1]
    C = math.gcd(T, GLA_CHUNK)
    n = T // C

    def blocks(a):
        return jnp.moveaxis(a.astype(jnp.float32).reshape(B, n, C, H, a.shape[-1]), 1, 0)

    causal = jnp.tril(jnp.ones((C, C), dtype=bool))[None, :, :, None, None]

    def step(S, inp):
        qc, kc, vc, ac = inp
        b = jnp.cumsum(ac, axis=1)
        diff = b[:, :, None] - b[:, None, :]
        decay = jnp.exp(jnp.where(causal, diff, -jnp.inf))
        scores = jnp.einsum('bihd,bjhd,bijhd->bhij', qc, kc, decay)
        o = (jnp.einsum('bhij,bjhv->bihv', scores, vc)
             + jnp.einsum('bihd,bhdv->bihv', qc * jnp.exp(b), S))
        b_last = b[:, -1]
        S = (jnp.exp(b_last)[..., None] * S
             + jnp.einsum('bjhd,bjhv->bhdv', kc * jnp.exp(b_last[:, None] - b), vc))
        return S, o

    S, o = lax.scan(step, s0.astype(jnp.float32), (blocks(q), blocks(k), blocks(v), blocks(log_a)))
    return jnp.moveaxis(o, 0, 1).reshape(B, T, H, DV), S

def gmlp_spatial(v, w_s, b_s):
    B, T, H, D = v.shape
    C = min(T, GMLP_CHUNK)
    n = T // C
    w = jnp.tril(w_s[:, :C, :C])
    out = jnp.einsum('hts,bnshd->bnthd', w, v.reshape(B, n, C, H, D))
    out = out + b_s[:, :C].T[None, None, :, :, None]
    return out.reshape(B, T, H, D)

def mixer(x, s0, w_in, w_a_up, b_a, gla_norm_g, gmlp_ln_g, gmlp_ln_b, w_s, b_s, gmlp_norm_g, w_out):
    B, T, _ = x.shape
    z = x @ w_in
    o1 = QK_WIDTH
    o2 = o1 + QK_WIDTH
    o3 = o2 + GLA_WIDTH
    o4 = o3 + GLA_WIDTH
    o5 = o4 + GLA_RANK
    o6 = o5 + GMLP_WIDTH
    q, k, v_a, g, a_lr, u, v_b = jnp.split(z, [o1, o2, o3, o4, o5, o6], axis=-1)
    log_a = jax.nn.log_sigmoid((a_lr @ w_a_up + b_a).astype(jnp.float32)) / GLA_TAU
    o_gla, s_new = gla_scan(
        q.reshape(B, T, GLA_HEADS, GLA_DK) * (GLA_DK ** -0.5),
        k.reshape(B, T, GLA_HEADS, GLA_DK),
        v_a.reshape(B, T, GLA_HEADS, GLA_DV),
        log_a.reshape(B, T, GLA_HEADS, GLA_DK),
        s0)
    o_gla = head_rmsnorm(o_gla, gla_norm_g) * jax.nn.silu(
        g.reshape(B, T, GLA_HEADS, GLA_DV).astype(jnp.float32))
    u = jax.nn.gelu(u)
    vg = layernorm(jax.nn.gelu(v_b), gmlp_ln_g, gmlp_ln_b)
    sgu = gmlp_spatial(vg.reshape(B, T, GMLP_HEADS, GMLP_DH), w_s, b_s)
    o_gmlp = head_rmsnorm(u.reshape(B, T, GMLP_HEADS, GMLP_DH) * sgu, gmlp_norm_g)
    merged = jnp.concatenate([o_gla.reshape(B, T, GLA_WIDTH),
                              o_gmlp.reshape(B, T, GMLP_WIDTH)], axis=-1).astype(x.dtype)
    return merged @ w_out, s_new.astype(s0.dtype), vg

def moe(h, w_router, router_bias, w_gate, w_up, w_down, ws_gate, ws_up, ws_down):
    B, T, D = h.shape
    t = h.reshape(B * T, D)
    N = t.shape[0]
    s = jax.nn.sigmoid((t @ w_router).astype(jnp.float32))
    sb = s + router_bias.astype(jnp.float32)
    grp = sb.reshape(N, N_GROUPS, N_EXPERTS // N_GROUPS)
    group_score = lax.top_k(grp, 2)[0].sum(-1)
    _, gidx = lax.top_k(group_score, TOPK_GROUPS)
    gmask = jnp.any(gidx[..., None] == jnp.arange(N_GROUPS), axis=-2)
    emask = jnp.repeat(gmask, N_EXPERTS // N_GROUPS, axis=-1)
    _, eidx = lax.top_k(jnp.where(emask, sb, -jnp.inf), TOP_K)
    sel = jnp.take_along_axis(s, eidx, axis=-1)
    wts = sel / sel.sum(-1, keepdims=True) * ROUTE_SCALE
    combine = jnp.zeros((N, N_EXPERTS), jnp.float32).at[jnp.arange(N)[:, None], eidx].set(wts)
    hid = jax.nn.silu(jnp.einsum('nd,edf->nef', t, w_gate)) * jnp.einsum('nd,edf->nef', t, w_up)
    hid = hid * combine[..., None].astype(hid.dtype)
    routed = jnp.einsum('nef,efd->nd', hid, w_down)
    shared = (jax.nn.silu(t @ ws_gate) * (t @ ws_up)) @ ws_down
    return (routed + shared).reshape(B, T, D)

def layer(x, s0, w_in, w_a_up, b_a, gla_norm_g, gmlp_ln_g, gmlp_ln_b, w_s, b_s, gmlp_norm_g,
          w_out, ln1_g, ln1_b, w_router, router_bias, w_gate, w_up, w_down,
          ws_gate, ws_up, ws_down, ln2_g, ln2_b):
    m, s_new, v_rows = mixer(x, s0, w_in, w_a_up, b_a, gla_norm_g, gmlp_ln_g, gmlp_ln_b,
                             w_s, b_s, gmlp_norm_g, w_out)
    h = layernorm(ALPHA * x + m, ln1_g, ln1_b)
    f = moe(h, w_router, router_bias, w_gate, w_up, w_down, ws_gate, ws_up, ws_down)
    y = layernorm(ALPHA * h + f, ln2_g, ln2_b)
    return y, s_new, v_rows

def setup_inputs(seed: int = 0) -> dict:
    key = jax.random.key(seed)
    ks = jax.random.split(key, 32)
    f32 = jnp.float32
    nrm = lambda k, shape, scale: jax.random.normal(k, shape, f32) * scale
    L = DEPTH
    col_scale = jnp.concatenate([
        jnp.ones((2 * QK_WIDTH,), f32), jnp.full((GLA_WIDTH,), BETA, f32),
        jnp.ones((GLA_WIDTH + GLA_RANK,), f32), jnp.full((GMLP_WIDTH,), BETA, f32),
        jnp.ones((GMLP_WIDTH,), f32)])
    return {
        'x_prompt': nrm(ks[0], (BATCH, SEQ, D_MODEL), 1.0),
        'x_sample': nrm(ks[1], (DEC_BATCH, DEC_SEQ, D_MODEL), 1.0),
        'state_gla': nrm(ks[2], (L, DEC_BATCH, GLA_HEADS, GLA_DK, GLA_DV), 0.5),
        'w_in': nrm(ks[3], (L, D_MODEL, N_IN), D_MODEL ** -0.5) * col_scale,
        'w_a_up': nrm(ks[4], (L, GLA_RANK, QK_WIDTH), GLA_RANK ** -0.5),
        'b_a': nrm(ks[5], (L, QK_WIDTH), 0.1),
        'gla_norm_g': 1.0 + nrm(ks[6], (L, GLA_HEADS, GLA_DV), 0.1),
        'gmlp_ln_g': 1.0 + nrm(ks[7], (L, GMLP_WIDTH), 0.1),
        'gmlp_ln_b': nrm(ks[8], (L, GMLP_WIDTH), 0.1),
        'w_s': nrm(ks[9], (L, GMLP_HEADS, GMLP_CHUNK, GMLP_CHUNK), GMLP_CHUNK ** -0.5),
        'b_s': 1.0 + nrm(ks[10], (L, GMLP_HEADS, GMLP_CHUNK), 0.1),
        'gmlp_norm_g': 1.0 + nrm(ks[11], (L, GMLP_HEADS, GMLP_DH), 0.1),
        'w_out': nrm(ks[12], (L, D_MIX, D_MODEL), D_MIX ** -0.5 * BETA),
        'ln1_g': 1.0 + nrm(ks[13], (L, D_MODEL), 0.1),
        'ln1_b': nrm(ks[14], (L, D_MODEL), 0.1),
        'w_router': nrm(ks[15], (L, D_MODEL, N_EXPERTS), D_MODEL ** -0.5),
        'router_bias': nrm(ks[16], (L, N_EXPERTS), 0.01),
        'w_gate': nrm(ks[17], (L, N_EXPERTS, D_MODEL, D_EXPERT), D_MODEL ** -0.5),
        'w_up': nrm(ks[18], (L, N_EXPERTS, D_MODEL, D_EXPERT), D_MODEL ** -0.5),
        'w_down': nrm(ks[19], (L, N_EXPERTS, D_EXPERT, D_MODEL), D_EXPERT ** -0.5 * BETA),
        'ws_gate': nrm(ks[20], (L, D_MODEL, D_SHARED), D_MODEL ** -0.5),
        'ws_up': nrm(ks[21], (L, D_MODEL, D_SHARED), D_MODEL ** -0.5),
        'ws_down': nrm(ks[22], (L, D_SHARED, D_MODEL), D_SHARED ** -0.5 * BETA),
        'ln2_g': 1.0 + nrm(ks[23], (L, D_MODEL), 0.1),
        'ln2_b': nrm(ks[24], (L, D_MODEL), 0.1),
    }

def reference(x_prompt, x_sample, state_gla, w_in, w_a_up, b_a, gla_norm_g, gmlp_ln_g, gmlp_ln_b,
              w_s, b_s, gmlp_norm_g, w_out, ln1_g, ln1_b, w_router, router_bias, w_gate, w_up,
              w_down, ws_gate, ws_up, ws_down, ln2_g, ln2_b):
    hp, hs = x_prompt, x_sample
    gla_p, gla_s, v_s = [], [], []
    for l in range(DEPTH):
        lw = (w_in[l], w_a_up[l], b_a[l], gla_norm_g[l], gmlp_ln_g[l], gmlp_ln_b[l], w_s[l], b_s[l],
              gmlp_norm_g[l], w_out[l], ln1_g[l], ln1_b[l], w_router[l], router_bias[l], w_gate[l],
              w_up[l], w_down[l], ws_gate[l], ws_up[l], ws_down[l], ln2_g[l], ln2_b[l])
        s0_prompt = jnp.zeros((hp.shape[0], GLA_HEADS, GLA_DK, GLA_DV), state_gla.dtype)
        hp, sp, _ = layer(hp, s0_prompt, *lw)
        hs, ss, vrows = layer(hs, state_gla[l], *lw)
        gla_p.append(sp)
        gla_s.append(ss)
        v_s.append(vrows)
    state_gla_prompt = jnp.stack(gla_p)
    state_gla_sample = jnp.stack(gla_s)
    state_gmlp_v_sample = jnp.stack(v_s)
    return (hp, hs, state_gla_prompt, state_gla_sample, state_gmlp_v_sample)


_drawn_inputs = setup_inputs


def setup_inputs(seed=0):
    import zlib

    import numpy as np

    out = dict(_drawn_inputs(seed))
    spreads = {}
    factors = {}
    for name, (base, spread) in spreads.items():
        noise = np.random.default_rng([zlib.crc32(name.encode()), seed]).standard_normal(out[name].shape)
        drawn = base * np.exp(spread * noise) if base else spread * noise
        out[name] = __import__('jax').numpy.asarray(drawn.astype(out[name].dtype))
    for name, factor in factors.items():
        out[name] = (out[name] * factor).astype(out[name].dtype)
    return out
```

```python
from contextlib import ExitStack

import concourse.bass as bass
from concourse import mybir

F32 = mybir.dt.float32
BF16 = mybir.dt.bfloat16
U32 = mybir.dt.uint32
ALU = mybir.AluOpType
ACT = mybir.ActivationFunctionType
AX = mybir.AxisListType

P = 128
BANK = 512
D = 1024
KT = D // P
FAR = 8192.0
HIT = 10000.0
NEG = -1.0e30


class Turns:

    def __init__(self, banks):
        self.banks, self.next, self.count, self.of = banks, 0, [0] * banks, {}

    def take(self, name, banks=1):
        got = []
        for _ in range(banks):
            b = self.next
            self.next = (b + 1) % self.banks
            self.count[b] += 1
            got.append((b, self.count[b]))
        self.of[name] = got


def hybrid_layer(nc, x_prompt, x_sample, state_gla, w_in, w_a_up, b_a, gla_norm_g, gmlp_ln_g, gmlp_ln_b,
                 w_s, b_s, gmlp_norm_g, w_out, ln1_g, ln1_b, w_router, router_bias, w_gate, w_up, w_down,
                 ws_gate, ws_up, ws_down, ln2_g, ln2_b,
                 y_prompt, y_sample, state_prompt, state_sample, v_sample):
    SEQ = x_prompt.shape[1]
    DB, DS = x_sample.shape[0], x_sample.shape[1]
    H, DK, DV = state_gla.shape[2:]
    RANK = w_a_up.shape[1]
    PAIRS = H // 2
    NE, FE = w_gate.shape[1], w_gate.shape[3]
    NG = 8
    GE = NE // NG
    TOPG = 4
    TOPK = 8
    CH = 64
    N = SEQ + DB * DS
    NT = SEQ // P + 1
    ROWS = [P] * (NT - 1) + [DB * DS]
    NS = DB * DS
    NCH = SEQ // CH
    ALPHA = 2.0 ** 0.25
    ROUTE_SCALE = 2.5
    PAIRROWS = N * TOPK
    EP = NE + 4
    AHEAD = 4
    MC = 5
    FK = FE // P
    OQ, OK_, OV, OG = 0, H * DK, 2 * H * DK, 2 * H * DK + H * DV
    OA = OG + H * DV
    OU = OA + RANK
    OVB = OU + 512
    assert ROWS[-1] == 64 and N <= 640 and FE == 256 and D == 1024

    with ExitStack() as ctx:
        def sb(name, shape, dt=F32):
            return ctx.enter_context(nc.sbuf_tensor(name, shape, dt))

        def sem(name):
            return ctx.enter_context(nc.semaphore(name))

        psum = ctx.enter_context(nc.psum_tensor("psum", [P, 8, BANK], F32))
        wring = sb("wring", [P, 2 * 6144])
        xT = sb("xT", [P, KT, N])
        x_sb = sb("x_sb", [P, NT, D])
        merged = sb("merged", [P, KT, N])
        arena = sb("arena", [P, 14848])
        ln_gb = sb("ln_gb", [P, 2, D])
        gln_gb = sb("gln_gb", [P, 2, 512])
        work = sb("work", [P, 4, BANK])
        ident = sb("ident", [P, P])
        mean_w = sb("mean_w", [P, P])
        ones_w = sb("ones_w", [P, P])
        before = sb("before", [P, P])
        cum_p = sb("cum_p", [P, 3, P])
        cum_s = sb("cum_s", [NS, 3, NS])
        mid_p = sb("mid_p", [P, P])
        mid_s = sb("mid_s", [NS, NS])
        upto = sb("upto", [P, P])
        tri8 = sb("tri8", [P, NG, NG])
        slot10k = sb("slot10k", [P, P])
        part = sb("part", [P, 1])
        seq_mask = sb("seq_mask", [NS, DB])
        wsT = sb("wsT", [P, H, P])
        wsT_s = sb("wsT_s", [NS, H, NS])
        bs_row = sb("bs_row", [1, H, P])
        bs_row_s = sb("bs_row_s", [1, H, NS])
        wr = sb("wr", [P, KT, NE])
        rbias = sb("rbias", [P, NE])
        wa = sb("wa", [RANK + 1, H * DK])
        alrT = sb("alrT", [RANK + 1, N])
        walr = sb("walr", [P, KT, RANK])
        gn_gla = sb("gn_gla", [P, H])
        gn_gmlp = sb("gn_gmlp", [P, H])
        eps5 = sb("eps5", [P, 1])
        eps6 = sb("eps6", [P, 1])
        stats = sb("stats", [P, 2, 6])
        mv = sb("mv", [P, NT, 2])
        rstd = sb("rstd", [P, NT])
        mv1 = sb("mv1", [P, NT, 2])
        rstd1 = sb("rstd1", [P, NT])
        ebl = sb("ebl", [P, PAIRS, NCH])
        ebl_s = sb("ebl_s", [P, PAIRS, DB])
        posm = sb("posm", [P, NT, EP])
        aux = sb("aux", [P, NT, EP, MC], BF16)
        slotrow = sb("slotrow", [P, EP])
        wt_all = sb("wt_all", [P, EP])
        row_all = sb("row_all", [P, EP])
        g_idx = sb("g_idx", [P, NT, TOPK], U32)
        crowded = sb("crowded", [1, 1], U32)
        meta = sb("meta", [P, MC])
        metaf = sb("metaf", [P, 2])
        idx = sb("idx", [P, 2], U32)
        yrow = sb("yrow", [P, 2], U32)

        h_dram = nc.dram_tensor("h_rows", (N, D), F32, kind="Internal").ap()
        y_dram = nc.dram_tensor("pair_rows", (PAIRROWS, D), F32, kind="Internal").ap()

        chunk = [wring[:, c * 4096:(c + 1) * 4096].rearrange("p (k n) -> p k n", k=KT) for c in range(3)]
        S0 = wring[:, 4096:4096 + 2048].rearrange("p (r b v) -> p r b v", r=PAIRS, b=DB)
        k2m = wring[0:NS, 6144:8192].rearrange("p (b n) -> p b n", b=DB)
        E = arena[:, 0:5120].rearrange("p (t r k n) -> p t r k n", t=NT, r=PAIRS, k=4)
        v_a = arena[:, 5120:7680].rearrange("p (t n) -> p t n", t=NT)
        v_b = arena[:, 7680:10240].rearrange("p (t n) -> p t n", t=NT)
        qkT = arena[:, 10240:12544].rearrange("p (f n) -> p f n", f=4)
        S = arena[:, 10240:12544].rearrange("p (c r v) -> p c r v", c=NCH + 1, r=PAIRS)
        la = arena[:, 12544:13824].rearrange("p (t n) -> p t n", t=NT)
        k2 = la
        scT = arena[:, 13824:14848].rearrange("p (u h n) -> p u h n", u=2, h=H)[:, :, :, :]
        hg = arena[:, 0:2048].rearrange("p (u n) -> p u n", u=2)
        hgT = arena[:, 2048:4096].rearrange("p (u n) -> p u n", u=2)
        y_sb = arena[:, 4096:6144].rearrange("p (u n) -> p u n", u=2)
        onehot = arena[:, 6144:6784].bitcast(BF16).rearrange("p (u t n) -> p u t n", u=2, t=NT)
        sg = arena[:, 6784:7296].rearrange("p (u n) -> p u n", u=2)
        hid = arena[:, 7296:7808].rearrange("p (u n) -> p u n", u=2)
        hidT = arena[:, 7808:8320].rearrange("p (u n) -> p u n", u=2)
        HALF = TOPK // 2
        rows_sb = [z.rearrange("p (j n) -> p j n", j=HALF) for z in
                   (arena[:, 8320:12416], arena[:, 0:4096], wring[:, 6144:10240])]
        mflat = merged[:, :, :].rearrange("p k n -> p (k n)")

        def scratch(n, count):
            return mflat[:, n * NT * NE:n * NT * NE + count]

        def gu_w(u):
            return wring[:, u * 6144:u * 6144 + 4096].rearrange("p (g k n) -> p g k n", g=2, k=KT)

        def wd_w(u):
            return wring[:, u * 6144 + 4096:(u + 1) * 6144].rearrange("p (k n) -> p k n", k=FK)

        def wd_flat(u):
            return wring[:, u * 6144 + 4096:(u + 1) * 6144]

        def gu_flat(u, g):
            return wring[:, u * 6144 + 2048 * g:u * 6144 + 2048 * (g + 1)]

        def tok(t):
            return slice(t * P, t * P + ROWS[t])

        bank_full = [sem(f"bank_full{b}") for b in range(8)]
        bank_empty = [sem(f"bank_empty{b}") for b in range(8)]
        x_loaded = [sem(f"x_loaded{t}") for t in range(NT)]
        small_loaded = sem("small_loaded")
        chunk_loaded = [sem(f"chunk_loaded{c}") for c in range(3)]
        walr_loaded, ln2_loaded, S0_loaded = sem("walr_loaded"), sem("ln2_loaded"), sem("S0_loaded")
        pool_step, dve_step, act_step = sem("pool_step"), sem("dve_step"), sem("act_step")
        pool_passed = sem("pool_passed")
        x_passed = sem("x_passed")
        consts_ready = sem("consts_ready")
        negabs_ready, softplus_ready, la_ready = sem("negabs_ready"), sem("softplus_ready"), sem("la_ready")
        vb_var, vb_std, vg_ready = sem("vb_var"), sem("vb_std"), sem("vg_ready")
        qk_ready, k2m_ready = sem("qk_ready"), sem("k2m_ready")
        sq_ready, gla_ready, gmlp_ready = sem("sq_ready"), sem("gla_ready"), sem("gmlp_ready")
        var1_ready, std1_ready, h_ready = sem("var1_ready"), sem("std1_ready"), sem("h_ready")
        s_ready, mask_ready, route_ready = sem("s_ready"), sem("mask_ready"), sem("route_ready")
        h_stored, out_stored = sem("h_stored"), sem("out_stored")
        gu_loaded = [sem(f"gu_loaded{u}") for u in range(2)]
        wd_loaded = [sem(f"wd_loaded{u}") for u in range(2)]
        gathered = [sem(f"gathered{u}") for u in range(2)]
        scattered = [sem(f"scattered{u}") for u in range(2)]
        gu_full, silu_ready, hid_ready = sem("gu_full"), sem("silu_ready"), sem("hid_ready")
        hidT_full, hidT_ready = sem("hidT_full"), sem("hidT_ready")
        y_full, yA_ready, yB_ready = sem("y_full"), sem("yA_ready"), sem("yB_ready")
        onehot_ready, meta_full, meta_taken = sem("onehot_ready"), sem("meta_full"), sem("meta_taken")
        idx_ready, hg_cleared = sem("idx_ready"), sem("hg_cleared")
        T_full, TA_ready, TB_ready = sem("T_full"), sem("TA_ready"), sem("TB_ready")
        x_loaded_w, x_onehot, x_meta, x_idx, x_gathered = (sem("x_loaded_w"), sem("x_onehot"), sem("x_meta"), sem("x_idx"),
                                                           sem("x_gathered"))
        x_T, x_hgT, x_gu, x_silu, x_hid = sem("x_T"), sem("x_hgT"), sem("x_gu"), sem("x_silu"), sem("x_hid")
        x_hidT_full, x_hidT, x_y, x_y_sb, x_stored = (sem("x_hidT_full"), sem("x_hidT"), sem("x_y"), sem("x_y_sb"),
                                                      sem("x_stored"))
        x_step, x_moved = sem("x_step"), sem("x_moved")
        rows_gathered = [sem(f"rows_gathered{n}") for n in range(3)]
        acc_ready, rows_added = sem("acc_ready"), sem("rows_added")
        var2_ready, std2_ready, out_ready = sem("var2_ready"), sem("std2_ready"), sem("out_ready")

        turns = Turns(8)
        for t in range(NT):
            turns.take(("xT", t, 0))
            turns.take(("xT", t, 1))
        turns.take("alr", 2)
        for f in range(4):
            turns.take(("qk", f), 2)
        for t in range(NT):
            turns.take(("pre", t))
        for t in range(NT):
            turns.take(("va", t))
        for t in range(NT):
            turns.take(("vb", t))
        for t in range(NT):
            turns.take(("cum", t), 2)
        for f in range(4):
            turns.take(("u", f), 2)
        for f in range(4):
            turns.take(("g", f), 2)
        turns.take("ws")
        turns.take("ws_s")
        for t in range(NT):
            turns.take(("k2", t))
        for c in range(NCH):
            turns.take(("U", c))
        for t in range(NT):
            turns.take(("sc", t), 2)
            turns.take(("o", t), 2)
            turns.take(("ms", t))
        turns.take("Us", 4)
        for t in range(NT):
            turns.take(("sgu", t))
            turns.take(("mg", t))
        for t in range(NT):
            turns.take(("m", t), 2)
        for t in range(NT):
            turns.take(("hT", t, 0))
            turns.take(("hT", t, 1))
        turns.take("logits")
        turns.take("pos")
        turns.take("cnt")
        turns.take("base")
        LAST = list(turns.count)

        def bank(name, n=0):
            return psum[:, turns.of[name][n][0], :]

        def claim(pe, name):
            for b, turn in turns.of[name]:
                if turn > 1:
                    pe.wait_ge(bank_empty[b], turn - 1)

        def filled(ins, name, n=0):
            ins.then_inc(bank_full[turns.of[name][n][0]], 1)

        def await_full(eng, name, n=0):
            b, turn = turns.of[name][n]
            eng.wait_ge(bank_full[b], turn)

        def emptied(ins, name, n=0):
            ins.then_inc(bank_empty[turns.of[name][n][0]], 1)

        def await_emptied(eng, name, n=0):
            b, turn = turns.of[name][n]
            eng.wait_ge(bank_empty[b], turn)

        def further_slots(eng, steps, before_them):
            eng.wait_ge(route_ready, 1)
            flag = eng.value_load(crowded[0:1, 0:1], min_val=0, max_val=1)
            with eng.If(flag > 0):
                before_them()
                with eng.Fori(0, NT - 1) as b:
                    if eng.engine == mybir.EngineType.DVE:
                        steps.move(b)
                    with eng.Fori(0, NE) as e:
                        n = b * NE + e + 1
                        steps(e, n)
                        eng.wait_ge(x_stored, 16 * n)
                        eng.sem_inc(x_passed, 1)

        SMALL = 16 + DB
        NCONST = 1

        block = ctx.enter_context(nc.Block())

        @block.sync
        def _(sp):
            for t in range(NT):
                src = x_prompt[0, tok(t), :] if t < NT - 1 else x_sample.rearrange("b s d -> (b s) d")
                sp.dma_start(x_sb[0:ROWS[t], t, :], src).then_inc(x_loaded[t], 16)
            w_rows = w_in[0].rearrange("(p k) n -> p k n", k=KT)
            sp.dma_start(walr[:, :, :], w_rows[:, :, OA:OA + RANK]).then_inc(walr_loaded, 16)
            sp.dma_start(chunk[0], w_rows[:, :, OQ:OQ + 512]).then_inc(chunk_loaded[0], 16)
            n = 0

            def small(dst, src):
                nonlocal n
                sp.dma_start(dst, src).then_inc(small_loaded, 16)
                n += 1

            small(wa[0:RANK, :], w_a_up[0])
            small(wa[RANK:RANK + 1, :], b_a)
            sp.dma_start(chunk[1], w_rows[:, :, OV:OV + 512]).then_inc(chunk_loaded[1], 16)
            sp.dma_start(chunk[2], w_rows[:, :, OVB:OVB + 512]).then_inc(chunk_loaded[2], 16)
            with nc.allow_non_contiguous_dma(reason="per-head gains, one column a head"):
                small(gn_gla[:, :], gla_norm_g[0].rearrange("h v -> v h"))
                small(gn_gmlp[:, :], gmlp_norm_g[0].rearrange("h v -> v h"))
            small(gln_gb[:, 0, :], gmlp_ln_g[0].partition_broadcast(P))
            small(gln_gb[:, 1, :], gmlp_ln_b[0].partition_broadcast(P))
            small(ln_gb[:, 0, :], ln1_g[0].partition_broadcast(P))
            small(ln_gb[:, 1, :], ln1_b[0].partition_broadcast(P))
            small(rbias[:, :], router_bias[0].partition_broadcast(P))
            small(work[:, 0, :].rearrange("p (h s) -> p h s", h=H), w_s[0].rearrange("h t s -> t h s"))
            sp.wait_ge(consts_ready, NCONST)
            for b in range(DB):
                small(work[b * DS:(b + 1) * DS, 1, 0:H * NS].rearrange("p (h s) -> p h s", h=H)[:, :, b * DS:(b + 1) * DS],
                      w_s[0, :, 0:DS, 0:DS].rearrange("h t s -> t h s"))
            small(bs_row[:, :, :], b_s)
            for h in range(H):
                small(bs_row_s[:, h, :].rearrange("o (b s) -> o b s", b=DB),
                      b_s[:, h, 0:DS].unsqueeze(1).to_broadcast([1, DB, DS]))
            small(wr[:, :, :], w_router[0].rearrange("(p k) n -> p k n", k=KT))
            assert n == SMALL, n
            await_full(sp, ("qk", 3), 0)
            await_full(sp, ("qk", 3), 1)
            sp.dma_start(chunk[0], w_rows[:, :, OU:OU + 512]).then_inc(chunk_loaded[0], 16)
            await_full(sp, ("va", NT - 1))
            sp.dma_start(chunk[1], w_rows[:, :, OG:OG + 512]).then_inc(chunk_loaded[1], 16)
            wo_rows = w_out[0].rearrange("(k p) n -> p k n", p=P)
            await_full(sp, ("vb", NT - 1))
            sp.dma_start(chunk[2], wo_rows[:, :, 0:512]).then_inc(chunk_loaded[2], 16)
            await_full(sp, ("u", 3), 0)
            await_full(sp, ("u", 3), 1)
            sp.dma_start(chunk[0], wo_rows[:, :, 512:1024]).then_inc(chunk_loaded[0], 16)
            await_full(sp, ("g", 3), 0)
            await_full(sp, ("g", 3), 1)
            for r in range(PAIRS):
                sp.dma_start(S0[:, r, :, :], state_gla[0, :, 2 * r:2 * r + 2].rearrange("b h k v -> (h k) b v")).then_inc(S0_loaded, 16)
            sp.wait_ge(vg_ready, NT)
            sp.dma_start(v_sample[0].rearrange("b s n -> (b s) n"), v_b[0:NS, NT - 1, :]).then_inc(out_stored, 16)
            await_emptied(sp, ("U", NCH - 1))
            sp.dma_start(state_prompt[0, 0].rearrange("(r h) k v -> (h k) r v", h=2), S[:, NCH, :, :]).then_inc(out_stored, 16)
            await_emptied(sp, "Us", 2 * PAIRS - 1)
            for r in range(PAIRS):
                sp.dma_start(state_sample[0, :, 2 * r:2 * r + 2].rearrange("b h k v -> (h k) b v"), S0[:, r, :, :]).then_inc(out_stored, 16)
            for t in range(NT):
                sp.wait_ge(h_ready, t + 1)
                sp.dma_start(h_dram[tok(t), :], x_sb[0:ROWS[t], t, :]).then_inc(h_stored, 16)
            sp.dma_start(ln_gb[:, 0, :], ln2_g[0].partition_broadcast(P)).then_inc(ln2_loaded, 16)
            sp.dma_start(ln_gb[:, 1, :], ln2_b[0].partition_broadcast(P)).then_inc(ln2_loaded, 16)

            def expert(w, e):
                return w[0, bass.ds(e, 1)].rearrange("o (p k) n -> p (o k n)", p=P)

            def load_gu(u, e):
                sp.dma_start(gu_flat(u, 0), expert(w_gate, e)).then_inc(gu_loaded[u], 16)
                sp.dma_start(gu_flat(u, 1), expert(w_up, e)).then_inc(gu_loaded[u], 16)

            def load_wd(u, e):
                sp.dma_start(wd_flat(u), expert(w_down, e)).then_inc(wd_loaded[u], 16)

            await_full(sp, ("m", NT - 1), 0)
            await_full(sp, ("m", NT - 1), 1)
            sp.wait_ge(out_stored, 16 * 4)
            for u in range(2):
                load_gu(u, u)
                load_wd(u, u)

            with sp.Fori(0, NE // 2 - 1) as j:
                for u in range(2):
                    sp.wait_ge(gu_full, 2 * j + (u + 1))
                    load_gu(u, 2 * j + (u + 2))
                    sp.wait_ge(y_full, 4 * j + 2 * (u + 1))
                    load_wd(u, 2 * j + (u + 2))
            sp.wait_ge(gu_full, NE - 1)
            sp.dma_start(gu_flat(0, 0), ws_gate[0].rearrange("(p k) n -> p (k n)", p=P)).then_inc(gu_loaded[0], 16)
            sp.dma_start(gu_flat(0, 1), ws_up[0].rearrange("(p k) n -> p (k n)", p=P)).then_inc(gu_loaded[0], 16)
            sp.wait_ge(y_full, 2 * (NE - 1))
            sp.dma_start(wd_flat(0), ws_down[0].rearrange("(p k) n -> p (k n)", p=P)).then_inc(wd_loaded[0], 16)

            def further(e, n):
                for g, w in enumerate((w_gate, w_up)):
                    sp.dma_start(gu_flat(1, g), expert(w, e)).then_inc(x_loaded_w, 16)
                sp.dma_start(wd_flat(1), expert(w_down, e)).then_inc(x_loaded_w, 16)

            further_slots(sp, further, lambda: sp.wait_ge(y_full, 2 * NE))
            for t in range(NT):
                sp.wait_ge(out_ready, t + 1)
                dst = y_prompt[0, tok(t), :] if t < NT - 1 else y_sample.rearrange("b s d -> (b s) d")
                sp.dma_start(dst, x_sb[0:ROWS[t], t, :]).then_inc(out_stored, 16)
            sp.wait_ge(out_stored, 16 * (4 + NT))

        @block.gpsimd
        def _(pool):
            count = [0]

            def link(ins):
                count[0] += 1
                ins.then_inc(pool_step, 1)
                pool.wait_ge(pool_step, count[0])

            def keep(view, pattern, base, cm, op=ALU.is_ge, fill=0.0):
                link(pool.affine_select(out=view, in_=view, pattern=pattern, compare_op=op, fill=fill,
                                        base=base, channel_multiplier=cm))

            pool.memset(work[:, 1, :], 0.0)
            pool.memset(alrT[:, :], 1.0)
            pool.memset(ones_w[:, :], 1.0)
            pool.memset(mean_w[:, :], 1.0 / P)
            pool.memset(eps5[:, :], 1e-5)
            pool.memset(eps6[:, :], 1e-6)
            pool.memset(mv[:, :, :], 1.0)
            pool.memset(mv1[:, :, :], 1.0)
            pool.memset(posm[:, :, :], 0.0)
            pool.memset(aux[:, :, :, :], 0.0)
            pool.memset(slotrow[:, :], 0.0)
            pool.memset(before[:, :], 1.0)
            pool.memset(upto[:, :], 1.0)
            pool.memset(cum_p[:, :, :], 1.0)
            pool.memset(cum_s[:, :, :], 1.0)
            pool.memset(mid_p[:, :], 1.0)
            pool.memset(mid_s[:, :], 1.0)
            pool.memset(tri8[:, :, :], 1.0)
            pool.memset(seq_mask[:, :], 1.0)
            pool.memset(scT[:, :, :, :], 0.0)
            link(pool.memset(ident[:, :], 0.0))
            keep(ident[:, :], [[-1, P]], 0, 1, ALU.not_equal, 1.0)
            keep(before[:, :], [[1, P]], -1, -1)
            keep(upto[:, :], [[1, P]], 0, -1)
            keep(tri8[:, :, :], [[1, NG], [-1, NG]], -1, 0)
            keep(seq_mask[:, :], [[-DS, DB]], 0, 1)
            keep(seq_mask[:, :], [[DS, DB]], DS - 1, -1)
            for cum, mid, n, c in ((cum_p, mid_p, P, CH), (cum_s, mid_s, NS, DS)):
                for kind in range(3):
                    v = cum[:, kind, :].rearrange("p (n c) -> p n c", c=c)
                    keep(v, [[-c, n // c], [0, c]], 0, 1)
                    keep(v, [[c, n // c], [0, c]], c - 1, -1)
                    if kind < 2:
                        keep(v, [[c, n // c], [1, c]], 0, -1)
                    else:
                        keep(v, [[-c, n // c], [-1, c]], -1, 1)
                v = mid[:, :].rearrange("p (n c) -> p n c", c=c)
                keep(v, [[-c, n // c], [0, c]], 0, 1)
                keep(v, [[c, n // c], [0, c]], c // 2 - 1, -1)
                link(pool.tensor_tensor(cum[:, 0, :], cum[:, 0, :], mid[:, :], ALU.subtract))
            link(pool.iota(slot10k[:, :], [[1, P]], base=int(HIT), channel_multiplier=0,
                           allow_small_or_imprecise_dtypes=True))
            link(pool.iota(part[:, :], [[0, 1]], base=0, channel_multiplier=1,
                           allow_small_or_imprecise_dtypes=True))
            for t in range(NT):
                link(pool.tensor_copy(aux[:, t, 0:NE, 0], part[:, 0:1].to_broadcast([P, NE])))
                link(pool.memset(aux[:, t, 0:NE, 1], t * P - FAR))
            pool.memset(g_idx[:, :, :], 0).then_inc(consts_ready, 1)

            await_emptied(pool, ("k2", NT - 1))
            await_full(pool, ("g", 3), 0)
            await_full(pool, ("g", 3), 1)
            pool.tensor_tensor(k2m, k2[0:NS, NT - 1, :].unsqueeze(1).to_broadcast([NS, DB, H * DK]),
                               seq_mask[:, :].unsqueeze(2).to_broadcast([NS, DB, H * DK]), ALU.mult).then_inc(k2m_ready, 1)

            pool.wait_ge(route_ready, 1)
            pool.memset(hg[:, :, :], 0.0).then_inc(hg_cleared, 1)
            pool.wait_ge(hg_cleared, 1)
            pool.wait_ge(h_stored, 16 * NT)

            last_token, last_pair = pool.to_reg(N - 1), pool.to_reg(PAIRROWS - 1)

            def gather(u, n):
                pool.wait_ge(idx_ready, n)
                pool.sem_inc(pool_passed, 1)
                pool.indirect_dma_start(hg[:, u, :], None, h_dram,
                                        bass.IndirectOffsetOnAxis(ap=idx[:, u:u + 1], axis=0),
                                        bounds_check=last_token, oob_is_err=False).then_inc(gathered[u], 16)

            def scatter(u, n):
                pool.wait_ge(yA_ready, n)
                pool.wait_ge(yB_ready, n)
                pool.sem_inc(pool_passed, 1)
                pool.indirect_dma_start(y_dram, bass.IndirectOffsetOnAxis(ap=yrow[:, u:u + 1], axis=0),
                                        y_sb[:, u, :], None, bounds_check=last_pair,
                                        oob_is_err=False).then_inc(scattered[u], 16)

            gather(0, 1)
            gather(1, 2)
            pool.wait_ge(T_full, 2)
            gather(0, 3)
            with pool.Fori(0, NE // 2 - 2) as j:
                for u in range(2):
                    pool.wait_ge(T_full, 4 * j + 2 * u + 4)
                    gather((u + 1) % 2, 2 * j + (u + 4))
                    scatter(u, 2 * j + (u + 1))
            for i in range(NE - 4, NE):
                if i + 3 < NE:
                    pool.wait_ge(T_full, 2 * (i + 2))
                    gather((i + 1) % 2, i + 4)
                scatter(i % 2, i + 1)
            for u in range(2):
                pool.wait_ge(scattered[u], 16 * (NE // 2))

            def further(e, n):
                pool.wait_ge(x_idx, n)
                pool.sem_inc(pool_passed, 1)
                pool.indirect_dma_start(hg[:, 0, :], None, h_dram, bass.IndirectOffsetOnAxis(ap=idx[:, 0:1], axis=0),
                                        bounds_check=last_token, oob_is_err=False).then_inc(x_gathered, 16)
                pool.wait_ge(x_y_sb, n)
                pool.sem_inc(pool_passed, 1)
                pool.indirect_dma_start(y_dram, bass.IndirectOffsetOnAxis(ap=yrow[:, 0:1], axis=0), y_sb[:, 0, :], None,
                                        bounds_check=last_pair, oob_is_err=False).then_inc(x_stored, 16)

            further_slots(pool, further, lambda: None)
            pool.wait_ge(gu_full, NE)
            pool.wait_ge(y_full, 2 * NE)
            for n in range(2 * NT):
                t, half = n // 2, n % 2
                if n >= 3:
                    pool.wait_ge(rows_added, n - 2)
                for k in range(HALF):
                    pool.indirect_dma_start(rows_sb[n % 3][0:ROWS[t], k, :], None, y_dram,
                                            bass.IndirectOffsetOnAxis(ap=g_idx[0:ROWS[t], t, HALF * half + k:HALF * half + k + 1], axis=0),
                                            bounds_check=last_pair, oob_is_err=False).then_inc(rows_gathered[n % 3], 16)

        @block.tensor
        def _(pe):
            pe.wait_ge(consts_ready, NCONST)

            def transposes(name, src, t):
                r = ROWS[t]
                for h in range(2):
                    claim(pe, (name, t, h))
                    for k in range(4):
                        ins = pe.transpose(bank((name, t, h))[:, k * P:k * P + r], src[0:r, t, 4 * h + k::KT], ident[0:r, 0:r])
                    filled(ins, (name, t, h))

            for t in range(NT):
                pe.wait_ge(x_loaded[t], 16)
                transposes("xT", x_sb, t)
            for t in range(NT):
                await_emptied(pe, ("xT", t, 0))
                await_emptied(pe, ("xT", t, 1))

            def feature_rows(name, w, m=P):
                claim(pe, name)
                for k in range(KT):
                    a = pe.matmul(bank(name, 0)[0:m, 0:SEQ], w(k), xT[:, k, 0:SEQ], start=(k == 0), stop=(k == KT - 1))
                    b = pe.matmul(bank(name, 1)[0:m, 0:NS], w(k), xT[:, k, SEQ:N], start=(k == 0), stop=(k == KT - 1))
                filled(a, name, 0)
                filled(b, name, 1)

            def token_rows(name, t, c):
                claim(pe, (name, t))
                for k in range(KT):
                    ins = pe.matmul(bank((name, t))[0:ROWS[t], :], xT[:, k, tok(t)], chunk[c][:, k, :],
                                    start=(k == 0), stop=(k == KT - 1))
                filled(ins, (name, t))

            pe.wait_ge(walr_loaded, 16)
            feature_rows("alr", lambda k: walr[:, k, :], RANK)
            pe.wait_ge(chunk_loaded[0], 16)
            for f in range(4):
                feature_rows(("qk", f), lambda k, f=f: chunk[0][:, k, f * P:(f + 1) * P])
            await_emptied(pe, "alr", 0)
            await_emptied(pe, "alr", 1)
            pe.wait_ge(small_loaded, 16 * SMALL)
            for t in range(NT):
                claim(pe, ("pre", t))
                filled(pe.matmul(bank(("pre", t))[0:ROWS[t], 0:H * DK], alrT[:, tok(t)], wa[:, :], start=True, stop=True), ("pre", t))
            pe.wait_ge(chunk_loaded[1], 16)
            for t in range(NT):
                token_rows("va", t, 1)
            pe.wait_ge(chunk_loaded[2], 16)
            for t in range(NT):
                token_rows("vb", t, 2)
            pe.wait_ge(la_ready, 2)
            for t in range(NT):
                r = ROWS[t]
                cum = cum_p if t < NT - 1 else cum_s
                claim(pe, ("cum", t))
                for p in range(PAIRS):
                    filled(pe.matmul(bank(("cum", t), p)[:, 0:3 * r], la[0:r, t, p * P:(p + 1) * P],
                                     cum[:, :, :].rearrange("p k n -> p (k n)"), start=True, stop=True), ("cum", t), p)
            pe.wait_ge(chunk_loaded[0], 32)
            for f in range(4):
                feature_rows(("u", f), lambda k, f=f: chunk[0][:, k, f * P:(f + 1) * P])
            pe.wait_ge(chunk_loaded[1], 32)
            for f in range(4):
                feature_rows(("g", f), lambda k, f=f: chunk[1][:, k, f * P:(f + 1) * P])
            claim(pe, "ws")
            for h in range(H):
                ins = pe.transpose(bank("ws")[:, h * P:(h + 1) * P], work[:, 0, h * P:(h + 1) * P], ident[:, :])
            filled(ins, "ws")
            claim(pe, "ws_s")
            for h in range(H):
                ins = pe.transpose(bank("ws_s")[0:NS, h * NS:(h + 1) * NS], work[0:NS, 1, h * NS:(h + 1) * NS], ident[0:NS, 0:NS])
            filled(ins, "ws_s")

            for t in range(NT):
                pe.wait_ge(qk_ready, PAIRS * (t + 1))
                claim(pe, ("k2", t))
                for p in range(PAIRS):
                    ins = pe.transpose(bank(("k2", t))[0:ROWS[t], p * P:(p + 1) * P], E[:, t, p, 3, 0:ROWS[t]], ident[:, :])
                filled(ins, ("k2", t))
            for t in range(NT):
                await_emptied(pe, ("va", t))
            for c in range(NCH):
                t, lo = c // 2, CH * (c % 2)
                await_emptied(pe, ("k2", t))
                claim(pe, ("U", c))
                for h in range(H):
                    ins = pe.matmul(bank(("U", c))[DK * (h % 2):DK * (h % 2) + DK, (h // 2) * DV:(h // 2 + 1) * DV],
                                    k2[lo:lo + CH, t, h * DK:(h + 1) * DK], v_a[lo:lo + CH, t, h * DV:(h + 1) * DV],
                                    start=True, stop=True)
                filled(ins, ("U", c))
            for t in range(NT):
                r = ROWS[t]
                claim(pe, ("sc", t))
                for h in (0, 2, 1, 3):
                    q = slice(DK * (h % 2), DK * (h % 2) + DK)
                    ins = pe.matmul(bank(("sc", t), h % 2)[0:r, h // 2 * P:h // 2 * P + r], E[q, t, h // 2, 2, 0:r],
                                    E[q, t, h // 2, 0, 0:r], start=True, stop=True)
                    if h > 1:
                        filled(ins, ("sc", t), h % 2)
                if t < NT - 1:
                    await_emptied(pe, ("U", 2 * t))
                else:
                    pe.wait_ge(S0_loaded, 16 * PAIRS)
                await_emptied(pe, ("sc", t), 0)
                await_emptied(pe, ("sc", t), 1)
                claim(pe, ("o", t))
                for h in (0, 2, 1, 3):
                    q = slice(DK * (h % 2), DK * (h % 2) + DK)
                    o = bank(("o", t), h % 2)[:, h // 2 * P:h // 2 * P + r]
                    ins = pe.matmul(o, v_a[:, t, h * DV:(h + 1) * DV], scT[:, t % 2, h, 0:r], start=True, stop=True,
                                    skip_group_check=True)
                    if t < NT - 1:
                        for c in range(2):
                            if 2 * t + c > 0:
                                ins = pe.matmul(o[:, c * CH:(c + 1) * CH], S[q, 2 * t + c, h // 2, :],
                                                E[q, t, h // 2, 1, c * CH:(c + 1) * CH], start=False, stop=True,
                                                skip_group_check=True)
                    else:
                        for b in range(DB):
                            ins = pe.matmul(o[:, b * DS:(b + 1) * DS], S0[q, h // 2, b, :],
                                            E[q, t, h // 2, 1, b * DS:(b + 1) * DS], start=False, stop=True,
                                            skip_group_check=True)
                    if h > 1:
                        filled(ins, ("o", t), h % 2)
                pe.wait_ge(sq_ready, 2 * (t + 1))
                claim(pe, ("ms", t))
                filled(pe.matmul(bank(("ms", t))[:, 0:H * r], mean_w[:, :], work[:, t % 2, 0:H * r], start=True, stop=True), ("ms", t))
            pe.wait_ge(k2m_ready, 1)
            claim(pe, "Us")
            for p in range(PAIRS):
                for b in range(DB):
                    for hh in range(2):
                        h = 2 * p + hh
                        ins = pe.matmul(bank("Us", 2 * p + b // 4)[DK * hh:DK * hh + DK, (b % 4) * DV:(b % 4 + 1) * DV],
                                        k2m[:, b, h * DK:(h + 1) * DK], v_a[0:NS, NT - 1, h * DV:(h + 1) * DV],
                                        start=True, stop=True)
                    if b % 4 == 3:
                        filled(ins, "Us", 2 * p + b // 4)
            await_emptied(pe, "ws")
            await_emptied(pe, "ws_s")
            for t in range(NT):
                r = ROWS[t]
                w, bs = (wsT, bs_row) if t < NT - 1 else (wsT_s, bs_row_s)
                pe.wait_ge(vg_ready, t + 1)
                claim(pe, ("sgu", t))
                pe.matmul(bank(("sgu", t))[:, 0:H * r], ones_w[0:1, :], bs[:, :, :].rearrange("o h n -> o (h n)"), start=True, stop=False,
                          skip_group_check=True)
                for h in range(H):
                    ins = pe.matmul(bank(("sgu", t))[:, h * r:(h + 1) * r], v_b[0:r, t, h * P:(h + 1) * P], w[:, h, :],
                                    start=False, stop=(h == H - 1), skip_group_check=True)
                filled(ins, ("sgu", t))
                pe.wait_ge(sq_ready, 2 * NT + t + 1)
                claim(pe, ("mg", t))
                filled(pe.matmul(bank(("mg", t))[:, 0:H * r], mean_w[:, :], work[:, (NT + t) % 2, 0:H * r], start=True, stop=True), ("mg", t))
            pe.wait_ge(chunk_loaded[2], 32)
            pe.wait_ge(chunk_loaded[0], 48)
            for t in range(NT):
                pe.wait_ge(gla_ready, t + 1)
                pe.wait_ge(gmlp_ready, t + 1)
                claim(pe, ("m", t))
                for n in range(2):
                    w = chunk[2] if n == 0 else chunk[0]
                    for k in range(KT):
                        ins = pe.matmul(bank(("m", t), n)[0:ROWS[t], :], merged[:, k, tok(t)], w[:, k, :],
                                        start=(k == 0), stop=(k == KT - 1))
                    filled(ins, ("m", t), n)
            for t in range(NT):
                pe.wait_ge(h_ready, t + 1)
                transposes("hT", x_sb, t)
            claim(pe, "logits")
            for t in range(NT):
                await_emptied(pe, ("hT", t, 0))
                await_emptied(pe, ("hT", t, 1))
                for k in range(KT):
                    ins = pe.matmul(bank("logits")[0:ROWS[t], t * NE:(t + 1) * NE], xT[:, k, tok(t)], wr[:, k, :],
                                    start=(k == 0), stop=(k == KT - 1))
            filled(ins, "logits")
            mask = scratch(1, NT * NE).rearrange("p (t e) -> p t e", t=NT)
            pe.wait_ge(mask_ready, 1)
            claim(pe, "pos")
            for t in range(NT):
                ins = pe.matmul(bank("pos")[:, t * NE:(t + 1) * NE], before[:, :], mask[:, t, :], start=True, stop=(t == 0))
                for s in range(t):
                    ins = pe.matmul(bank("pos")[:, t * NE:(t + 1) * NE], ones_w[:, :], mask[:, s, :], start=False, stop=(s == t - 1))
            filled(ins, "pos")
            claim(pe, "cnt")
            for t in range(NT):
                ins = pe.matmul(bank("cnt")[0:NE, 0:P], mask[:, t, :], ones_w[:, :], start=(t == 0), stop=(t == NT - 1))
            filled(ins, "cnt")
            await_emptied(pe, "cnt")
            claim(pe, "base")
            filled(pe.matmul(bank("base")[:, 0:NE], scratch(2, P)[0:NE, :], before[0:NE, 0:NE], start=True, stop=True), "base")
            for b in range(8):
                pe.wait_ge(bank_empty[b], LAST[b])

            def gate_up(u, loads):
                pe.wait_ge(gu_loaded[u], loads)
                for k in range(KT):
                    ins = pe.matmul(psum[:, u, :], hgT[:, u, k * P:(k + 1) * P], gu_w(u)[:, :, k, :], start=(k == 0), stop=(k == KT - 1))
                ins.then_inc(gu_full, 1)

            def hid_transpose(u, rows):
                for k in range(FK):
                    ins = pe.transpose(psum[:, 6, k * P:k * P + rows], hid[0:rows, u, k::FK], ident[0:rows, 0:rows])
                ins.then_inc(hidT_full, 1)

            def down(u, s, rows):
                for n in range(2):
                    for k in range(FK):
                        ins = pe.matmul(psum[0:rows, 4 + n, :], hidT[:, u, k * P:k * P + rows], wd_w(s)[:, k, n * 512:(n + 1) * 512],
                                        start=(k == 0), stop=(k == FK - 1))
                    ins.then_inc(y_full, 1)

            def tell(u, e):
                for t in range(NT):
                    ins = pe.matmul(psum[:, 7, 0:MC], onehot[:, u, t, :], aux[:, t, bass.ds(e, 1), :].rearrange("p o c -> p (o c)"),
                                    start=(t == 0), stop=(t == NT - 1))
                ins.then_inc(meta_full, 1)

            def turn_rows(u):
                for h in range(2):
                    for k in range(4):
                        ins = pe.transpose(psum[:, 2 + h, k * P:(k + 1) * P], hg[:, u, 4 * h + k::KT], ident[:, :])
                    ins.then_inc(T_full, 1)

            for e in range(AHEAD):
                pe.wait_ge(onehot_ready, e + 1)
                if e:
                    pe.wait_ge(meta_taken, e)
                tell(e % 2, e)
                if e == AHEAD - 2:
                    pe.wait_ge(gathered[0], 16)
                    turn_rows(0)
            pe.wait_ge(gathered[1], 16)
            pe.wait_ge(TA_ready, 1)
            pe.wait_ge(TB_ready, 1)
            turn_rows(1)
            pe.wait_ge(TA_ready, 1)
            pe.wait_ge(TB_ready, 1)
            gate_up(0, 32)

            def expert_steps(u, j):
                i = 2 * j + u
                first = isinstance(j, int) and i == 0
                left = NE - i if isinstance(j, int) else NE
                pe.wait_ge(hid_ready, i + 1)
                if not first:
                    pe.wait_ge(hidT_ready, i)
                hid_transpose(u, P)
                if left > 1:
                    pe.wait_ge(TA_ready, i + 2)
                    pe.wait_ge(TB_ready, i + 2)
                    gate_up(1 - u, 32 * (j + 1 + u))
                pe.wait_ge(hidT_ready, i + 1)
                pe.wait_ge(wd_loaded[u], 16 * (j + 1))
                if not first:
                    pe.wait_ge(yA_ready, i)
                    pe.wait_ge(yB_ready, i)
                down(u, u, P)
                if left > AHEAD:
                    pe.wait_ge(onehot_ready, i + AHEAD + 1)
                    pe.wait_ge(meta_taken, i + AHEAD)
                    tell(u, i + AHEAD)
                if left > 2:
                    pe.wait_ge(gathered[u], 16 * (j + 2))
                    turn_rows(u)

            expert_steps(0, 0)
            expert_steps(1, 0)
            with pe.Fori(1, NE // 2 - 2) as j:
                expert_steps(0, j)
                expert_steps(1, j)
            for j in range(NE // 2 - 2, NE // 2):
                expert_steps(0, j)
                expert_steps(1, j)

            def further(e, n):
                pe.wait_ge(x_onehot, n)
                for t in range(NT):
                    ins = pe.matmul(psum[:, 7, 0:MC], onehot[:, 0, t, :], aux[:, t, bass.ds(e, 1), :].rearrange("p o c -> p (o c)"),
                                    start=(t == 0), stop=(t == NT - 1))
                ins.then_inc(x_meta, 1)
                pe.wait_ge(x_gathered, 16 * n)
                for k in range(KT):
                    ins = pe.transpose(psum[:, 2 + k // 4, k % 4 * P:(k % 4 + 1) * P], hg[:, 0, k::KT], ident[:, :])
                ins.then_inc(x_T, 1)
                pe.wait_ge(x_hgT, n)
                pe.wait_ge(x_loaded_w, 48 * n)
                for k in range(KT):
                    ins = pe.matmul(psum[:, 0, :], hgT[:, 0, k * P:(k + 1) * P], gu_w(1)[:, :, k, :], start=(k == 0), stop=(k == KT - 1))
                ins.then_inc(x_gu, 1)
                pe.wait_ge(x_hid, n)
                for k in range(FK):
                    ins = pe.transpose(psum[:, 6, k * P:(k + 1) * P], hid[:, 0, k::FK], ident[:, :])
                ins.then_inc(x_hidT_full, 1)
                pe.wait_ge(x_hidT, n)
                for c in range(2):
                    for k in range(FK):
                        ins = pe.matmul(psum[:, 4 + c, :], hidT[:, 0, k * P:(k + 1) * P], wd_w(1)[:, k, c * 512:(c + 1) * 512],
                                        start=(k == 0), stop=(k == FK - 1))
                ins.then_inc(x_y, 1)

            def banks_read():
                pe.wait_ge(yA_ready, NE)
                pe.wait_ge(yB_ready, NE)

            further_slots(pe, further, banks_read)

            def shared_gu(t):
                pe.wait_ge(hid_ready, NE + t - 1)
                pe.wait_ge(gu_loaded[0], 32 * (NE // 2 + 1))
                r = ROWS[t]
                for k in range(KT):
                    ins = pe.matmul(psum[0:r, t % 2, :], xT[:, k, tok(t)], gu_w(0)[:, :, k, :], start=(k == 0), stop=(k == KT - 1))
                ins.then_inc(gu_full, 1)

            shared_gu(0)
            for t in range(NT):
                if t + 1 < NT:
                    shared_gu(t + 1)
                pe.wait_ge(hid_ready, NE + t + 1)
                pe.wait_ge(hidT_ready, NE + t)
                hid_transpose(t % 2, ROWS[t])
                pe.wait_ge(hidT_ready, NE + t + 1)
                pe.wait_ge(wd_loaded[0], 16 * (NE // 2 + 1))
                if t:
                    pe.wait_ge(acc_ready, t)
                else:
                    pe.wait_ge(yA_ready, NE)
                    pe.wait_ge(yB_ready, NE)
                down(t % 2, 0, ROWS[t])

        @block.scalar
        def _(act):
            count = [0]

            def link(ins):
                count[0] += 1
                ins.then_inc(act_step, 1)
                act.wait_ge(act_step, count[0])

            def heads(view, r):
                return view.rearrange("p (h n) -> p h n", h=4)[:, :, 0:r]

            act.wait_ge(consts_ready, NCONST)
            for t in range(NT):
                await_full(act, ("xT", t, 0))
                emptied(act.activation(xT[:, 0:4, tok(t)], heads(bank(("xT", t, 0)), ROWS[t]), ACT.Copy), ("xT", t, 0))

            def features(name, out, func):
                await_full(act, name, 0)
                emptied(act.activation(out[:, 0:SEQ], bank(name, 0), func), name, 0)
                await_full(act, name, 1)
                emptied(act.activation(out[:, SEQ:N], bank(name, 1)[:, 0:NS], func), name, 1)

            for f in (2, 3):
                features(("qk", f), qkT[:, f, :], ACT.Copy)
            for n, (r, cols) in enumerate(((P, slice(0, (NT - 1) * 256)), (NS, slice((NT - 1) * 256, NT * 256)))):
                tmp = arena[0:r, cols]
                act.wait_ge(negabs_ready, n + 1)
                link(act.activation(tmp, tmp, ACT.Exp))
                act.activation(tmp, tmp, ACT.Ln, bias=ones_w[0:r, 0:1]).then_inc(softplus_ready, 1)
            for t in range(NT):
                await_full(act, ("vb", t))
                emptied(act.activation(v_b[0:ROWS[t], t, :], bank(("vb", t))[0:ROWS[t], :], ACT.Gelu_apprx_tanh), ("vb", t))
            for t in range(NT):
                r = ROWS[t]
                for p in range(PAIRS):
                    c = bank(("cum", t), p)[:, 0:3 * r].rearrange("p (k n) -> p k n", k=3)
                    await_full(act, ("cum", t), p)
                    act.activation(E[:, t, p, 0:2, 0:r], c[:, 0:2, :], ACT.Exp, scale=1.0 / 16)
                    act.activation(E[:, t, p, 2, 0:r], c[:, 0, :], ACT.Exp, scale=-1.0 / 16)
                    emptied(act.activation(E[:, t, p, 3, 0:r], c[:, 2, :], ACT.Exp, scale=1.0 / 16), ("cum", t), p)
            act.wait_ge(vb_var, 1)
            act.activation(rstd[:, :], mv[:, :, 1], ACT.Sqrt, bias=eps5[:, 0:1]).then_inc(vb_std, 1)
            for f in range(4):
                features(("u", f), merged[:, 4 + f, :], ACT.Gelu_apprx_tanh)
            for f in range(4):
                features(("g", f), merged[:, f, :], ACT.Silu)
            for t in range(NT):
                await_full(act, ("k2", t))
                emptied(act.activation(k2[0:ROWS[t], t, :], bank(("k2", t))[0:ROWS[t], 0:256], ACT.Copy), ("k2", t))

            def root(name, t, n):
                w = 4 * ROWS[t]
                await_full(act, (name, t))
                emptied(act.activation(work[:, 2 + n % 2, 0:w], bank((name, t))[:, 0:w], ACT.Sqrt, bias=eps6[:, 0:1]), (name, t))

            for t in range(NT):
                r = ROWS[t]
                for odd in range(2):
                    await_full(act, ("o", t), odd)
                    act.activation(work[:, t % 2, 0:4 * r].rearrange("p (h n) -> p h n", h=4)[:, odd::2, :],
                                   heads(bank(("o", t), odd), r)[:, 0:2, :], ACT.Square).then_inc(sq_ready, 1)
                root("ms", t, t)
            for t in range(NT):
                r = ROWS[t]
                await_emptied(act, ("sgu", t))
                act.activation(work[:, (NT + t) % 2, 0:4 * r].rearrange("p (h n) -> p h n", h=4), merged[:, 4:8, tok(t)],
                               ACT.Square).then_inc(sq_ready, 1)
                root("mg", t, NT + t)
            for t in range(NT):
                act.wait_ge(var1_ready, t + 1)
                act.activation(rstd1[0:ROWS[t], t:t + 1], mv1[0:ROWS[t], t, 1:2], ACT.Sqrt,
                               bias=eps5[0:ROWS[t], 0:1]).then_inc(std1_ready, 1)
            for t in range(NT):
                await_full(act, ("hT", t, 0))
                emptied(act.activation(xT[:, 0:4, tok(t)], heads(bank(("hT", t, 0)), ROWS[t]), ACT.Copy), ("hT", t, 0))
            s = scratch(0, NT * NE)
            await_full(act, "logits")
            act.activation(s[:, 0:(NT - 1) * NE], bank("logits")[:, 0:(NT - 1) * NE], ACT.Sigmoid).then_inc(s_ready, 1)
            emptied(act.activation(s[0:NS, (NT - 1) * NE:], bank("logits")[0:NS, (NT - 1) * NE:NT * NE], ACT.Sigmoid), "logits")

            def silu(u, n, rows=P):
                act.wait_ge(gu_full, n)
                act.activation(sg[0:rows, u, :], psum[0:rows, u, 0:FE], ACT.Silu).then_inc(silu_ready, 1)

            def rows_half(u, n):
                act.wait_ge(T_full, n)
                act.activation(hgT[:, u, 0:512], psum[:, 2, :], ACT.Copy).then_inc(TA_ready, 1)

            rows_half(0, 1)
            rows_half(1, 3)
            silu(0, 1)

            def expert_steps(u, j):
                i = 2 * j + u
                left = NE - i if isinstance(j, int) else NE
                if left > 1:
                    silu(1 - u, i + 2)
                if not (isinstance(j, int) and j == 0):
                    act.wait_ge(scattered[u], 16 * j)
                act.wait_ge(y_full, 2 * i + 1)
                act.activation(y_sb[:, u, 0:512], psum[:, 4, :], ACT.Copy).then_inc(yA_ready, 1)
                if left > 2:
                    rows_half(u, 2 * i + 5)

            expert_steps(0, 0)
            expert_steps(1, 0)
            with act.Fori(1, NE // 2 - 1) as j:
                expert_steps(0, j)
                expert_steps(1, j)
            expert_steps(0, NE // 2 - 1)
            expert_steps(1, NE // 2 - 1)

            def further(e, n):
                act.wait_ge(x_T, n)
                act.activation(hgT[:, 0, :], psum[:, 2:4, :].rearrange("p b n -> p (b n)"), ACT.Copy).then_inc(x_hgT, 1)
                act.wait_ge(x_gu, n)
                act.activation(sg[:, 0, :], psum[:, 0, 0:FE], ACT.Silu).then_inc(x_silu, 1)
                act.wait_ge(x_y, n)
                act.activation(y_sb[:, 0, :], psum[:, 4:6, :].rearrange("p b n -> p (b n)"), ACT.Copy).then_inc(x_y_sb, 1)

            further_slots(act, further, lambda: act.wait_ge(scattered[0], 16 * (NE // 2)))
            silu(0, NE + 1)
            for t in range(NT):
                if t + 1 < NT:
                    silu((t + 1) % 2, NE + t + 2, ROWS[t + 1])
                act.wait_ge(var2_ready, t + 1)
                act.activation(rstd1[0:ROWS[t], t:t + 1], mv1[0:ROWS[t], t, 1:2], ACT.Sqrt,
                               bias=eps5[0:ROWS[t], 0:1]).then_inc(std2_ready, 1)

        @block.vector
        def _(dve):
            count = [0]

            def link(ins):
                count[0] += 1
                ins.then_inc(dve_step, 1)
                dve.wait_ge(dve_step, count[0])

            def heads(view, r):
                return view.rearrange("p (h n) -> p h n", h=4)[:, :, 0:r]

            link(dve.memset(v_a[NS:P, NT - 1, :], 0.0))
            dve.wait_ge(consts_ready, NCONST)
            for t in range(NT):
                await_full(dve, ("xT", t, 1))
                emptied(dve.tensor_copy(xT[:, 4:8, tok(t)], heads(bank(("xT", t, 1)), ROWS[t])), ("xT", t, 1))
            await_full(dve, "alr", 0)
            emptied(dve.tensor_copy(alrT[0:RANK, 0:SEQ], bank("alr", 0)[0:RANK, :]), "alr", 0)
            await_full(dve, "alr", 1)
            emptied(dve.tensor_copy(alrT[0:RANK, SEQ:N], bank("alr", 1)[0:RANK, 0:NS]), "alr", 1)
            for f in (0, 1):
                await_full(dve, ("qk", f), 0)
                emptied(dve.tensor_scalar(qkT[:, f, 0:SEQ], bank(("qk", f), 0), DK ** -0.5, None, ALU.mult), ("qk", f), 0)
                await_full(dve, ("qk", f), 1)
                emptied(dve.tensor_scalar(qkT[:, f, SEQ:N], bank(("qk", f), 1)[:, 0:NS], DK ** -0.5, None, ALU.mult), ("qk", f), 1)
            for t in range(NT):
                await_full(dve, ("pre", t))
                emptied(dve.tensor_copy(la[0:ROWS[t], t, :], bank(("pre", t))[0:ROWS[t], 0:256]), ("pre", t))
            await_emptied(dve, ("pre", NT - 1))
            await_emptied(dve, ("pre", NT - 2))
            parts = ((P, slice(0, (NT - 1) * 256)), (NS, slice((NT - 1) * 256, NT * 256)))
            laf = arena[:, 12544:13824]
            for r, cols in parts:
                dve.scalar_tensor_tensor(out=arena[0:r, cols], in0=laf[0:r, cols], scalar=-1.0, in1=laf[0:r, cols],
                                         op0=ALU.mult, op1=ALU.min).then_inc(negabs_ready, 1)
            for n, (r, cols) in enumerate(parts):
                dve.wait_ge(softplus_ready, n + 1)
                dve.scalar_tensor_tensor(out=laf[0:r, cols], in0=laf[0:r, cols], scalar=0.0, in1=arena[0:r, cols],
                                         op0=ALU.min, op1=ALU.subtract).then_inc(la_ready, 1)
            for t in range(NT):
                await_full(dve, ("va", t))
                emptied(dve.tensor_copy(v_a[0:ROWS[t], t, :], bank(("va", t))[0:ROWS[t], :]), ("va", t))
            for t in range(NT):
                r = ROWS[t]
                await_emptied(dve, ("vb", t))
                link(dve.bn_stats(stats[0:r, 0, :], v_b[0:r, t, :]))
                ins = dve.bn_aggr(mv[0:r, t, :], stats[0:r, 0, :])
                link(ins) if t < NT - 1 else ins.then_inc(vb_var, 1)
            dve.wait_ge(small_loaded, 16 * SMALL)
            for t in range(NT):
                r = ROWS[t]
                await_emptied(dve, ("cum", t), 0)
                await_emptied(dve, ("cum", t), 1)
                if t < NT - 1:
                    link(dve.tensor_copy(ebl[:, :, 2 * t:2 * t + 2], E[:, t, :, 1, CH - 1::CH]))
                else:
                    link(dve.tensor_copy(ebl_s[:, :, :], E[:, t, :, 1, DS - 1:NS:DS]))
                for p in range(PAIRS):
                    for kind, f in ((0, p), (2, 2 + p)):
                        e = E[:, t, p, kind:kind + 2, 0:r]
                        if (kind, f) == (2, 2 + p):
                            await_emptied(dve, ("qk", f), 0)
                            await_emptied(dve, ("qk", f), 1)
                        ins = dve.scalar_tensor_tensor(out=e, in0=e, scalar=1e30, in1=qkT[:, f, tok(t)].unsqueeze(1).to_broadcast([P, 2, r]),
                                                       op0=ALU.min, op1=ALU.mult)
                    ins.then_inc(qk_ready, 1)
            dve.wait_ge(vb_std, 1)
            link(dve.reciprocal(rstd[:, :], rstd[:, :]))
            for t in range(NT):
                r = ROWS[t]
                v = v_b[0:r, t, :]
                link(dve.tensor_scalar(v, v, mv[0:r, t, 0:1], rstd[0:r, t:t + 1], ALU.subtract, ALU.mult))
                link(dve.tensor_tensor(v, v, gln_gb[0:r, 0, :], ALU.mult))
                dve.tensor_tensor(v, v, gln_gb[0:r, 1, :], ALU.add).then_inc(vg_ready, 1)
            for f in range(4):
                await_emptied(dve, ("g", f), 0)
                await_emptied(dve, ("g", f), 1)
                link(dve.tensor_scalar(merged[:, f, :], merged[:, f, :], gn_gla[:, f:f + 1], None, ALU.mult))
            await_full(dve, "ws")
            emptied(dve.tensor_tensor(wsT[:, :, :], bank("ws").rearrange("p (h n) -> p h n", h=H),
                                      upto[:, :].unsqueeze(1).to_broadcast([P, H, P]), ALU.mult), "ws")
            await_full(dve, "ws_s")
            emptied(dve.tensor_tensor(wsT_s[:, :, :], bank("ws_s")[0:NS, 0:H * NS].rearrange("p (h n) -> p h n", h=H),
                                      upto[0:NS, 0:NS].unsqueeze(1).to_broadcast([NS, H, NS]), ALU.mult), "ws_s")
            for c in range(NCH):
                await_full(dve, ("U", c))
                if c == 0:
                    emptied(dve.tensor_copy(S[:, 1, :, :], bank(("U", c))[:, 0:256].rearrange("p (r v) -> p r v", r=PAIRS)), ("U", c))
                    await_emptied(dve, ("U", c))
                    continue
                for p in range(PAIRS):
                    ins = dve.scalar_tensor_tensor(out=S[:, c + 1, p, :], in0=S[:, c, p, :], scalar=ebl[:, p, c:c + 1],
                                                   in1=bank(("U", c))[:, p * DV:(p + 1) * DV], op0=ALU.mult, op1=ALU.add)
                emptied(ins, ("U", c))
                await_emptied(dve, ("U", c))

            def rms(name, t, n):
                w = work[:, 2 + n % 2, 0:4 * ROWS[t]]
                await_emptied(dve, (name, t))
                link(dve.reciprocal(w, w))
                return w.rearrange("p (h n) -> p h n", h=4)

            for t in range(NT):
                r = ROWS[t]
                causal = (cum_p if t < NT - 1 else cum_s)[:, 1, :].bitcast(U32)
                if t == NT - 1:
                    link(dve.memset(scT[:, t % 2, :, 0:r], 0.0))
                for odd in range(2):
                    await_full(dve, ("sc", t), odd)
                    emptied(dve.copy_predicated(scT[0:r, t % 2, odd::2, 0:r], causal.unsqueeze(1).to_broadcast([r, 2, r]),
                                                heads(bank(("sc", t), odd)[0:r, :], r)[:, 0:2, :]), ("sc", t), odd)
                for odd in range(2):
                    m = merged[:, odd:4:2, tok(t)]
                    dve.wait_ge(sq_ready, 2 * t + odd + 1)
                    emptied(dve.tensor_tensor(m, m, heads(bank(("o", t), odd), r)[:, 0:2, :], ALU.mult), ("o", t), odd)
                w = rms("ms", t, t)
                m = merged[:, 0:4, tok(t)]
                await_emptied(dve, ("o", t), 0)
                await_emptied(dve, ("o", t), 1)
                dve.tensor_tensor(m, m, w, ALU.mult).then_inc(gla_ready, 1)
            for p in range(PAIRS):
                link(dve.tensor_tensor(S0[:, p, :, :], S0[:, p, :, :], ebl_s[:, p, :].unsqueeze(2).to_broadcast([P, DB, DV]), ALU.mult))
                for half in range(2):
                    await_full(dve, "Us", 2 * p + half)
                    ins = dve.tensor_tensor(S0[:, p, 4 * half:4 * half + 4, :], S0[:, p, 4 * half:4 * half + 4, :],
                                            bank("Us", 2 * p + half).rearrange("p (b v) -> p b v", b=4), ALU.add)
                    emptied(ins, "Us", 2 * p + half)
                    await_emptied(dve, "Us", 2 * p + half)
            for t in range(NT):
                r = ROWS[t]
                m = merged[:, 4:8, tok(t)]
                for f in range(4):
                    if t == 0:
                        await_emptied(dve, ("u", f), 0)
                        await_emptied(dve, ("u", f), 1)
                await_full(dve, ("sgu", t))
                emptied(dve.tensor_tensor(m, m, bank(("sgu", t))[:, 0:H * r].rearrange("p (h n) -> p h n", h=H), ALU.mult), ("sgu", t))
                w = rms("mg", t, NT + t)
                for h in range(H):
                    ins = dve.scalar_tensor_tensor(out=merged[:, 4 + h, tok(t)], in0=merged[:, 4 + h, tok(t)], scalar=gn_gmlp[:, h:h + 1],
                                                   in1=w[:, h, :], op0=ALU.mult, op1=ALU.mult)
                ins.then_inc(gmlp_ready, 1)

            def norm_stats(t, ready):
                r = ROWS[t]
                for n in range(2):
                    link(dve.bn_stats(stats[0:r, n, :], x_sb[0:r, t, n * 512:(n + 1) * 512]))
                dve.bn_aggr(mv1[0:r, t, :], stats[0:r, :, :].rearrange("p a b -> p (a b)")).then_inc(ready, 1)

            def norm(t, std, ready):
                r = ROWS[t]
                x = x_sb[0:r, t, :]
                dve.wait_ge(std, t + 1)
                link(dve.reciprocal(rstd1[0:r, t:t + 1], rstd1[0:r, t:t + 1]))
                link(dve.tensor_scalar(x, x, mv1[0:r, t, 0:1], rstd1[0:r, t:t + 1], ALU.subtract, ALU.mult))
                link(dve.tensor_tensor(x, x, ln_gb[0:r, 0, :], ALU.mult))
                dve.tensor_tensor(x, x, ln_gb[0:r, 1, :], ALU.add).then_inc(ready, 1)

            for t in range(NT):
                r = ROWS[t]
                for n in range(2):
                    await_full(dve, ("m", t), n)
                    x = x_sb[0:r, t, n * 512:(n + 1) * 512]
                    emptied(dve.scalar_tensor_tensor(out=x, in0=x, scalar=ALPHA, in1=bank(("m", t), n)[0:r, :],
                                                     op0=ALU.mult, op1=ALU.add), ("m", t), n)
                    await_emptied(dve, ("m", t), n)
                norm_stats(t, var1_ready)
                if t:
                    norm(t - 1, std1_ready, h_ready)
            norm(NT - 1, std1_ready, h_ready)
            for t in range(NT):
                await_full(dve, ("hT", t, 1))
                emptied(dve.tensor_copy(xT[:, 4:8, tok(t)], heads(bank(("hT", t, 1)), ROWS[t])), ("hT", t, 1))

            def grp(n):
                return scratch(n, NT * NG)

            def all3(view):
                return view.rearrange("p (t e) -> p t e", t=NT)

            s, mask, counts, sbias = scratch(0, NT * NE), scratch(1, NT * NE), scratch(2, P), scratch(3, NT * NE)
            t1, t2 = scratch(4, NT * NE), scratch(5, NT * NE)
            m1, m2, cnt2, gs = (scratch(6, 4 * NT * NG)[:, n * NT * NG:(n + 1) * NT * NG] for n in range(4))
            m8 = scratch(7, 8)
            rows1 = scratch(8, NT * NE)
            sums = scratch(7, 8 + NT)[:, 8:8 + NT]
            last = slice((NT - 1) * NE, NT * NE)

            def by8(view):
                return view.rearrange("p (g e) -> p g e", e=GE)

            def over8(view):
                return view.unsqueeze(2).to_broadcast([P, NT * NG, GE])

            await_full(dve, "logits")
            link(dve.memset(s[NS:P, last], 0.0))
            dve.wait_ge(s_ready, 1)
            await_emptied(dve, "logits")
            link(dve.tensor_tensor(all3(sbias), all3(s), rbias[:, :].unsqueeze(1).to_broadcast([P, NT, NE]), ALU.add))
            link(dve.tensor_reduce(m1, by8(sbias), AX.X, ALU.max))
            link(dve.tensor_tensor(by8(t1), by8(sbias), over8(m1), ALU.is_equal))
            link(dve.tensor_reduce(cnt2, by8(t1), AX.X, ALU.add))
            link(dve.scalar_tensor_tensor(out=t1, in0=t1, scalar=NEG, in1=sbias, op0=ALU.mult, op1=ALU.add))
            link(dve.tensor_reduce(m2, by8(t1), AX.X, ALU.max))
            link(dve.tensor_scalar(cnt2, cnt2, 1.5, NEG, ALU.is_lt, ALU.mult))
            link(dve.tensor_tensor(cnt2, cnt2, m1, ALU.add))
            link(dve.tensor_tensor(m2, m2, cnt2, ALU.max))
            link(dve.tensor_tensor(gs, m1, m2, ALU.add))
            g4 = [NT, NG, NG]
            this = gs.rearrange("p (t g) -> p t g", t=NT).unsqueeze(3).to_broadcast([P] + g4)
            other = gs.rearrange("p (t g) -> p t g", t=NT).unsqueeze(2).to_broadcast([P] + g4)
            v1, v2 = (v.rearrange("p (t g o) -> p t g o", t=NT, g=NG) for v in (t1, t2))
            link(dve.tensor_tensor(v1, other, this, ALU.is_equal))
            link(dve.tensor_tensor(v1, v1, tri8[:, :, :].unsqueeze(1).to_broadcast([P] + g4), ALU.mult))
            link(dve.tensor_tensor(v2, other, this, ALU.is_gt))
            link(dve.tensor_tensor(t1, t1, t2, ALU.add))
            link(dve.tensor_reduce(m1, by8(t1), AX.X, ALU.add))
            link(dve.tensor_scalar(m1, m1, TOPG - 0.5, NEG, ALU.is_ge, ALU.mult))
            link(dve.tensor_tensor(by8(sbias), by8(sbias), over8(m1), ALU.add))
            for t in range(NT):
                c = slice(t * NE, (t + 1) * NE)
                link(dve.max(m8, sbias[:, c]))
                link(dve.match_replace(t1[:, c], m8, sbias[:, c], 4 * NEG))
            link(dve.tensor_tensor(mask, sbias, t1, ALU.not_equal))
            dve.memset(mask[NS:P, last], 0.0).then_inc(mask_ready, 1)
            dve.wait_ge(mask_ready, 1)
            link(dve.tensor_tensor(t2, s, mask, ALU.mult))
            link(dve.tensor_reduce(sums, all3(t2), AX.X, ALU.add))
            link(dve.memset(sums[NS:P, NT - 1:NT], 1.0))
            link(dve.reciprocal(sums, sums))
            link(dve.tensor_tensor(all3(t2), all3(t2), sums.unsqueeze(2).to_broadcast([P, NT, NE]), ALU.mult))
            link(dve.tensor_scalar(t2, t2, ROUTE_SCALE, None, ALU.mult))
            w = all3(t2)
            link(dve.tensor_copy(aux[:, :, 0:NE, 2], w))
            link(dve.tensor_tensor(w, w, aux[:, :, 0:NE, 2], ALU.subtract))
            link(dve.tensor_copy(aux[:, :, 0:NE, 3], w))
            link(dve.tensor_tensor(w, w, aux[:, :, 0:NE, 3], ALU.subtract))
            link(dve.tensor_copy(aux[:, :, 0:NE, 4], w))
            await_full(dve, "cnt")
            emptied(dve.tensor_copy(counts[0:NE, :], bank("cnt")[0:NE, 0:P]), "cnt")
            await_full(dve, "pos")
            emptied(dve.tensor_copy(rows1, bank("pos")[:, 0:NT * NE]), "pos")
            await_emptied(dve, "pos")
            link(dve.scalar_tensor_tensor(out=posm[:, :, 0:NE], in0=all3(mask), scalar=HIT, in1=all3(rows1), op0=ALU.mult, op1=ALU.add))
            await_full(dve, "base")
            emptied(dve.tensor_copy(t1[:, 0:NE], bank("base")[:, 0:NE]), "base")
            await_emptied(dve, "base")
            link(dve.tensor_scalar(slotrow[:, 0:NE], t1[:, 0:NE], part[:, 0:1], None, ALU.add))
            link(dve.tensor_tensor(t2[0:1, 0:NE - 1], t1[0:1, 1:NE], t1[0:1, 0:NE - 1], ALU.subtract))
            link(dve.tensor_scalar(t2[0:1, NE - 1:NE], t1[0:1, NE - 1:NE], -1.0, float(PAIRROWS), ALU.mult, ALU.add))
            link(dve.tensor_reduce(t2[0:1, NE:NE + 1], t2[0:1, 0:NE], AX.X, ALU.max))
            link(dve.tensor_scalar(crowded[:, :], t2[0:1, NE:NE + 1], P + 0.5, None, ALU.is_gt))
            link(dve.tensor_scalar(t1[:, 0:NE], t1[:, 0:NE], 1.0, None, ALU.add))
            link(dve.tensor_tensor(all3(rows1), all3(rows1), t1[:, 0:NE].unsqueeze(1).to_broadcast([P, NT, NE]), ALU.add))
            link(dve.tensor_tensor(rows1, rows1, mask, ALU.mult))
            for t in range(NT):
                link(dve.max(m8, rows1[:, t * NE:(t + 1) * NE]))
                link(dve.tensor_scalar(g_idx[0:ROWS[t], t, :], m8[0:ROWS[t], :], -1.0, None, ALU.add))
            ins = dve.tensor_copy(t1[:, 0:1], part[:, 0:1])
            ins.then_inc(route_ready, 1)

            base = count[0]

            class Chain:

                def __init__(self, start, j, per, of=dve_step):
                    self.start, self.j, self.per, self.n, self.sem = start, j, per, 0, of

                def __call__(self, ins):
                    self.n += 1
                    ins.then_inc(self.sem, 1)
                    dve.wait_ge(self.sem, self.start + self.j * self.per + self.n)

            def one_hot(u, e):
                dve.tensor_tensor(onehot[:, u, :, :], posm[:, :, bass.ds(e, 1)].to_broadcast([P, NT, P]),
                                  slot10k[:, :].unsqueeze(1).to_broadcast([P, NT, P]), ALU.is_equal).then_inc(onehot_ready, 1)

            def told(u, e, chain):
                dve.wait_ge(meta_full, e + 1)
                dve.tensor_copy(meta[:, :], psum[:, 7, 0:MC]).then_inc(meta_taken, 1)
                dve.wait_ge(meta_taken, e + 1)
                dve.scalar_tensor_tensor(out=wt_all[:, bass.ds(e, 1)], in0=meta[:, 2:3], scalar=meta[:, 3:4], in1=meta[:, 4:5],
                                         op0=ALU.add, op1=ALU.add)
                chain(dve.tensor_tensor(metaf[:, 0:1], meta[:, 0:1], meta[:, 1:2], ALU.add))
                chain(dve.tensor_scalar(metaf[:, 1:2], metaf[:, 0:1], -1.0, FAR, ALU.is_ge, ALU.mult))
                dve.tensor_tensor(row_all[:, bass.ds(e, 1)], metaf[:, 1:2], slotrow[:, bass.ds(e, 1)], ALU.add)
                dve.tensor_scalar(idx[:, u:u + 1], metaf[:, 0:1], FAR, None, ALU.add).then_inc(idx_ready, 1)

            def rows_half(u, n, m):
                dve.wait_ge(T_full, n)
                dve.tensor_copy(hgT[:, u, 512:1024], psum[:, 3, :]).then_inc(TB_ready, 1)

            def hidden(u, n, e):
                dve.wait_ge(silu_ready, n)
                dve.scalar_tensor_tensor(out=hid[:, u, :], in0=sg[:, u, :], scalar=wt_all[:, bass.ds(e, 1)],
                                         in1=psum[:, u, FE:2 * FE], op0=ALU.mult, op1=ALU.mult).then_inc(hid_ready, 1)

            one_hot(0, 0)
            one_hot(1, 1)
            chain = Chain(count[0], 0, 0)
            told(0, 0, chain)
            one_hot(0, 2)
            told(1, 1, chain)
            one_hot(1, 3)
            rows_half(0, 2, 0)
            told(0, 2, chain)
            one_hot(0, 4)
            rows_half(1, 4, 0)
            told(1, 3, chain)
            hidden(0, 1, 0)
            base = count[0] + chain.n

            def expert_steps(u, j, chain):
                i = 2 * j + u
                left = NE - i if isinstance(j, int) else NE
                dve.wait_ge(hidT_full, i + 1)
                dve.tensor_copy(hidT[:, u, :], psum[:, 6, 0:FK * P]).then_inc(hidT_ready, 1)
                if left > AHEAD + 1:
                    one_hot(1 - u, i + AHEAD + 1)
                if left > 1:
                    hidden(1 - u, i + 2, i + 1)
                if not (isinstance(j, int) and j == 0):
                    dve.wait_ge(scattered[u], 16 * j)
                chain(dve.tensor_copy(yrow[:, u:u + 1], row_all[:, bass.ds(i, 1)]))
                dve.wait_ge(y_full, 2 * i + 2)
                dve.tensor_copy(y_sb[:, u, 512:1024], psum[:, 5, :]).then_inc(yB_ready, 1)
                if left > 2:
                    rows_half(u, 2 * i + 6, i + 3)
                if left > AHEAD:
                    told(u, i + AHEAD, chain)

            chain = Chain(base, 0, 0)
            expert_steps(0, 0, chain)
            expert_steps(1, 0, chain)
            base += chain.n
            PER = chain.n
            with dve.Fori(1, NE // 2 - 3) as j:
                chain = Chain(base - PER, j, PER)
                expert_steps(0, j, chain)
                expert_steps(1, j, chain)
                assert chain.n == PER
            chain = Chain(base + (NE // 2 - 4) * PER, 0, 0)
            for j in range(NE // 2 - 3, NE // 2):
                expert_steps(0, j, chain)
                expert_steps(1, j, chain)
            count[0] = base + (NE // 2 - 4) * PER + chain.n

            class Further:

                def move(self, b):
                    dve.tensor_scalar(posm[:, :, 0:NE], posm[:, :, 0:NE], -float(P), None, ALU.add)
                    dve.tensor_scalar(slotrow[:, 0:NE], slotrow[:, 0:NE], float(P), None, ALU.add).then_inc(x_moved, 1)
                    dve.wait_ge(x_moved, b + 1)
                    dve.sem_inc(x_passed, 1)

                def __call__(self, e, n):
                    chain = Chain(0, n - 1, 5, x_step)
                    dve.tensor_tensor(onehot[:, 0, :, :], posm[:, :, bass.ds(e, 1)].to_broadcast([P, NT, P]),
                                      slot10k[:, :].unsqueeze(1).to_broadcast([P, NT, P]), ALU.is_equal).then_inc(x_onehot, 1)
                    dve.wait_ge(x_meta, n)
                    chain(dve.tensor_copy(meta[:, :], psum[:, 7, 0:MC]))
                    chain(dve.scalar_tensor_tensor(out=wt_all[:, 0:1], in0=meta[:, 2:3], scalar=meta[:, 3:4], in1=meta[:, 4:5],
                                                   op0=ALU.add, op1=ALU.add))
                    chain(dve.tensor_tensor(metaf[:, 0:1], meta[:, 0:1], meta[:, 1:2], ALU.add))
                    chain(dve.tensor_scalar(metaf[:, 1:2], metaf[:, 0:1], -1.0, FAR, ALU.is_ge, ALU.mult))
                    chain(dve.tensor_tensor(yrow[:, 0:1], metaf[:, 1:2], slotrow[:, bass.ds(e, 1)], ALU.add))
                    dve.tensor_scalar(idx[:, 0:1], metaf[:, 0:1], FAR, None, ALU.add).then_inc(x_idx, 1)
                    dve.wait_ge(x_silu, n)
                    dve.scalar_tensor_tensor(out=hid[:, 0, :], in0=sg[:, 0, :], scalar=wt_all[:, 0:1], in1=psum[:, 0, FE:2 * FE],
                                             op0=ALU.mult, op1=ALU.mult).then_inc(x_hid, 1)
                    dve.wait_ge(x_hidT_full, n)
                    dve.tensor_copy(hidT[:, 0, :], psum[:, 6, 0:FK * P]).then_inc(x_hidT, 1)

            def rows_stored():
                for u in range(2):
                    dve.wait_ge(scattered[u], 16 * (NE // 2))

            further_slots(dve, Further(), rows_stored)

            def shared_hidden(t):
                r = ROWS[t]
                dve.wait_ge(silu_ready, NE + t + 1)
                dve.tensor_tensor(hid[0:r, t % 2, :], sg[0:r, t % 2, :], psum[0:r, t % 2, FE:2 * FE], ALU.mult).then_inc(hid_ready, 1)

            shared_hidden(0)
            dve.wait_ge(ln2_loaded, 32)
            for t in range(NT):
                r = ROWS[t]
                if t + 1 < NT:
                    shared_hidden(t + 1)
                dve.wait_ge(hidT_full, NE + t + 1)
                dve.tensor_copy(hidT[:, t % 2, :].rearrange("p (k n) -> p k n", k=FK)[:, :, 0:r],
                                psum[:, 6, 0:FK * P].rearrange("p (k n) -> p k n", k=FK)[:, :, 0:r]).then_inc(hidT_ready, 1)
                dve.wait_ge(y_full, 2 * (NE + t + 1))
                for n in range(2):
                    x = x_sb[0:r, t, n * 512:(n + 1) * 512]
                    ins = dve.scalar_tensor_tensor(out=x, in0=x, scalar=ALPHA, in1=psum[0:r, 4 + n, :], op0=ALU.mult, op1=ALU.add)
                ins.then_inc(acc_ready, 1)
                dve.wait_ge(acc_ready, t + 1)
                for half in range(2):
                    n = 2 * t + half
                    dve.wait_ge(rows_gathered[n % 3], 16 * HALF * (n // 3 + 1))
                    for k in range(HALF):
                        ins = dve.tensor_tensor(x_sb[0:r, t, :], x_sb[0:r, t, :], rows_sb[n % 3][0:r, k, :], ALU.add)
                        if k < HALF - 1:
                            link(ins)
                    ins.then_inc(rows_added, 1)
                    dve.wait_ge(rows_added, n + 1)
                norm_stats(t, var2_ready)
                norm(t, std2_ready, out_ready)


_INS = ["x_prompt", "x_sample", "state_gla", "w_in", "w_a_up", "b_a", "gla_norm_g", "gmlp_ln_g", "gmlp_ln_b",
        "w_s", "b_s", "gmlp_norm_g", "w_out", "ln1_g", "ln1_b", "w_router", "router_bias", "w_gate", "w_up",
        "w_down", "ws_gate", "ws_up", "ws_down", "ln2_g", "ln2_b"]
_OUTS = [(1, 512, 1024), (8, 8, 1024), (1, 1, 4, 64, 128), (1, 8, 4, 64, 128), (1, 8, 8, 512)]


def kernel(**inputs):
    import numpy as _np
    import concourse.bacc as _bacc
    from concourse.bass_utils import run_bass_kernel_spmd as _run

    nc = _bacc.Bacc("TRN2", target_bir_lowering=False, num_devices=1)
    arrays, args = {}, []
    for name in _INS:
        a = _np.ascontiguousarray(inputs[name])
        arrays[f"in_{name}_dram"] = a
        args.append(nc.dram_tensor(f"in_{name}_dram", a.shape, mybir.dt.from_np(a.dtype), kind="ExternalInput").ap())
    for i, shape in enumerate(_OUTS):
        args.append(nc.dram_tensor(f"out_{i}_dram", shape, F32, kind="ExternalOutput").ap())
    hybrid_layer(nc, *args)
    r = _run(nc, [arrays], core_ids=[0])
    return tuple(r.results[0][f"out_{i}_dram"] for i in range(len(_OUTS)))
```

```python
from contextlib import ExitStack

import concourse.bass as bass
from concourse import mybir

F32 = mybir.dt.float32
BF16 = mybir.dt.bfloat16
U32 = mybir.dt.uint32
ALU = mybir.AluOpType
ACT = mybir.ActivationFunctionType
AX = mybir.AxisListType

P = 128
BANK = 512
D = 1024
KT = D // P
HIT = 10000.0
NEG = -1.0e30


class Turns:

    def __init__(self, banks):
        self.banks, self.next, self.count, self.of = banks, 0, [0] * banks, {}

    def take(self, name, banks=1):
        got = []
        for _ in range(banks):
            b = self.next
            self.next = (b + 1) % self.banks
            self.count[b] += 1
            got.append((b, self.count[b]))
        self.of[name] = got


def hybrid_layer(nc, x_prompt, x_sample, state_gla, w_in, w_a_up, b_a, gla_norm_g, gmlp_ln_g, gmlp_ln_b,
                 w_s, b_s, gmlp_norm_g, w_out, ln1_g, ln1_b, w_router, router_bias, w_gate, w_up, w_down,
                 ws_gate, ws_up, ws_down, ln2_g, ln2_b,
                 y_prompt, y_sample, state_prompt, state_sample, v_sample):
    SEQ = x_prompt.shape[1]
    DB, DS = x_sample.shape[0], x_sample.shape[1]
    H, DK, DV = state_gla.shape[2:]
    RANK = w_a_up.shape[1]
    PAIRS = H // 2
    NE, FE = w_gate.shape[1], w_gate.shape[3]
    NG = 8
    GE = NE // NG
    TOPG = 4
    CH = 64
    N = SEQ + DB * DS
    NT = SEQ // P + 1
    ROWS = [P] * (NT - 1) + [DB * DS]
    NS = DB * DS
    NCH = SEQ // CH
    HALVES = (slice(0, N // 2), slice(N // 2, N))
    NH = N // 2
    ALPHA = 2.0 ** 0.25
    ROUTE_SCALE = 2.5
    EP = NE + 4
    AHEAD = 4
    MC = 5
    FK = FE // P
    OQ, OV, OG = 0, 2 * H * DK, 2 * H * DK + H * DV
    OA = OG + H * DV
    OU = OA + RANK
    OVB = OU + 512
    assert NT == 5 and NE % 4 == 0 and ROWS[-1] == 64 and N <= 640 and FE == 256 and D == 1024

    with ExitStack() as ctx:
        def sb(name, shape, dt=F32):
            return ctx.enter_context(nc.sbuf_tensor(name, shape, dt))

        def sem(name):
            return ctx.enter_context(nc.semaphore(name))

        psum = ctx.enter_context(nc.psum_tensor("psum", [P, 8, BANK], F32))
        wring = sb("wring", [P, 2 * 6144])
        xT = sb("xT", [P, KT, N])
        x_sb = sb("x_sb", [P, NT, D])
        merged = sb("merged", [P, KT, N])
        arena = sb("arena", [P, 14848])
        ln_gb = sb("ln_gb", [P, 2, D])
        gln_gb = sb("gln_gb", [P, 2, 512])
        work = sb("work", [P, 4, BANK])
        ident = sb("ident", [P, P])
        mean_w = sb("mean_w", [P, P])
        ones_w = sb("ones_w", [P, P])
        before = sb("before", [P, P])
        cum_p = sb("cum_p", [P, 3, P])
        cum_s = sb("cum_s", [NS, 3, NS])
        mid_p = sb("mid_p", [P, P])
        mid_s = sb("mid_s", [NS, NS])
        upto = sb("upto", [P, P])
        tri8 = sb("tri8", [P, NG, NG])
        slot10k = sb("slot10k", [P, P])
        part = sb("part", [P, 1])
        seq_mask = sb("seq_mask", [NS, DB])
        wsT = sb("wsT", [P, H, P])
        wsT_s = sb("wsT_s", [NS, H, NS])
        bs = sb("bs", [P, H, P])
        wr = sb("wr", [P, KT, NE])
        rbias = sb("rbias", [P, NE])
        wa = sb("wa", [P, H * DK])
        alrT = sb("alrT", [P, N])
        walr = sb("walr", [P, KT, 32])
        gn_gla = sb("gn_gla", [P, H])
        gn_gmlp = sb("gn_gmlp", [P, H])
        eps5 = sb("eps5", [P, 1])
        eps6 = sb("eps6", [P, 1])
        stats = sb("stats", [P, 2, 6])
        mv = sb("mv", [P, NT, 2])
        rstd = sb("rstd", [P, NT])
        mv1 = sb("mv1", [P, NT, 2])
        rstd1 = sb("rstd1", [P, NT])
        ebl = sb("ebl", [P, PAIRS, NCH])
        ebl_s = sb("ebl_s", [P, PAIRS, DB])
        posm = sb("posm", [P, NT, EP])
        aux = sb("aux", [P, NT, EP, MC], BF16)
        wt_all = sb("wt_all", [P, EP])
        row_all = sb("row_all", [P, EP])
        crowded = sb("crowded", [1, 1], U32)
        meta = sb("meta", [P, MC])
        metaf = sb("metaf", [P, 2])
        idx = sb("idx", [P, 2], U32)
        yrow = sb("yrow", [P, 2], U32)

        h_dram = nc.dram_tensor("h_rows", (N, D), F32, kind="Internal").ap()
        sum_dram = nc.dram_tensor("sum_rows", (N + P, D), F32, kind="Internal").ap()

        chunk = [wring[:, c * 4096:(c + 1) * 4096].rearrange("p (k n) -> p k n", k=KT) for c in range(3)]
        S0 = wring[:, 4096:4096 + 2048].rearrange("p (r b v) -> p r b v", r=PAIRS, b=DB)
        k2m = wring[0:NS, 6144:8192].rearrange("p (b n) -> p b n", b=DB)
        E = arena[:, 0:5120].rearrange("p (t r k n) -> p t r k n", t=NT, r=PAIRS, k=4)
        v_a = arena[:, 5120:7680].rearrange("p (t n) -> p t n", t=NT)
        v_b = arena[:, 7680:10240].rearrange("p (t n) -> p t n", t=NT)
        qkT = arena[:, 10240:12544].rearrange("p (f n) -> p f n", f=4)
        S = arena[:, 10240:12544].rearrange("p (c r v) -> p c r v", c=NCH + 1, r=PAIRS)
        la = arena[:, 12544:13824].rearrange("p (t n) -> p t n", t=NT)
        k2 = la
        scT = arena[:, 13824:14848].rearrange("p (u h n) -> p u h n", u=2, h=H)
        hg = arena[:, 0:2048].rearrange("p (u n) -> p u n", u=2)
        hgT = arena[:, 2048:4096].rearrange("p (u n) -> p u n", u=2)
        y_sb = arena[:, 4096:6144].rearrange("p (u n) -> p u n", u=2)
        onehot = arena[:, 6144:6784].bitcast(BF16).rearrange("p (u t n) -> p u t n", u=2, t=NT)
        sg = arena[:, 6784:7296].rearrange("p (u n) -> p u n", u=2)
        hid = arena[:, 7296:7808].rearrange("p (u n) -> p u n", u=2)
        hidT = arena[:, 7808:8320].rearrange("p (u n) -> p u n", u=2)
        ws_gu = arena[:, 8320:12416].rearrange("p (g k n) -> p g k n", g=2, k=KT)
        ws_d = arena[:, 12416:14464].rearrange("p (k n) -> p k n", k=FK)
        sh_silu = merged[:, :, :].rearrange("p k n -> p (k n)")[:, 9 * NT * NE:9 * NT * NE + FK * N].rearrange("p (f n) -> p f n", f=FK)
        sh_hid = work[:, :, :].rearrange("p a n -> p (a n)")[:, 0:FK * N].rearrange("p (f n) -> p f n", f=FK)

        def sh_rows(t):
            if t < NT - 1:
                return xT[:, :, :].rearrange("p k n -> p (k n)")[:, t * D:(t + 1) * D]
            return gln_gb[:, :, :].rearrange("p a n -> p (a n)")

        mflat = merged[:, :, :].rearrange("p k n -> p (k n)")

        def scratch(n, count):
            return mflat[:, n * NT * NE:n * NT * NE + count]

        def gu_w(u):
            return wring[:, u * 6144:u * 6144 + 4096].rearrange("p (g k n) -> p g k n", g=2, k=KT)

        def wd_flat(s):
            if s < 2:
                return wring[:, s * 6144 + 4096:(s + 1) * 6144]
            return arena[:, 8320 + (s - 2) * 2048:8320 + (s - 1) * 2048]

        def wd_w(s):
            return wd_flat(s).rearrange("p (k n) -> p k n", k=FK)

        def gu_flat(u, g):
            return wring[:, u * 6144 + 2048 * g:u * 6144 + 2048 * (g + 1)]

        def tok(t):
            return slice(t * P, t * P + ROWS[t])

        bank_full = [sem(f"bank_full{b}") for b in range(8)]
        bank_empty = [sem(f"bank_empty{b}") for b in range(8)]
        x_loaded = [sem(f"x_loaded{t}") for t in range(NT)]
        small_loaded = sem("small_loaded")
        chunk_loaded = [sem(f"chunk_loaded{c}") for c in range(3)]
        q_loaded = sem("q_loaded")
        walr_loaded, ln2_loaded, S0_loaded = sem("walr_loaded"), sem("ln2_loaded"), sem("S0_loaded")
        pool_step, dve_step, act_step = sem("pool_step"), sem("dve_step"), sem("act_step")
        pool_passed = sem("pool_passed")
        x_passed = sem("x_passed")
        gate_cleared, first_consts, consts_ready = sem("gate_cleared"), sem("first_consts"), sem("consts_ready")
        negabs_ready, softplus_ready, la_ready = sem("negabs_ready"), sem("softplus_ready"), sem("la_ready")
        vb_var, vb_std, vg_ready = sem("vb_var"), sem("vb_std"), sem("vg_ready")
        qk_ready, k2m_ready = sem("qk_ready"), sem("k2m_ready")
        u_gated = sem("u_gated")
        sq_gla, sq_gmlp, gla_ready, gmlp_ready = sem("sq_gla"), sem("sq_gmlp"), sem("gla_ready"), sem("gmlp_ready")
        var1_ready, std1_ready, h_ready = sem("var1_ready"), sem("std1_ready"), sem("h_ready")
        mask_ready, route_ready = sem("mask_ready"), sem("route_ready")
        h_stored = [sem(f"h_stored{t}") for t in range(NT)]
        spare_stored, out_stored = sem("spare_stored"), sem("out_stored")
        gu_loaded = [sem(f"gu_loaded{u}") for u in range(2)]
        wd_loaded = [sem(f"wd_loaded{s}") for s in range(4)]
        gathered = [sem(f"gathered{u}") for u in range(2)]
        added = sem("added")
        gu_full, silu_ready, hid_ready = sem("gu_full"), sem("silu_ready"), sem("hid_ready")
        hidT_full, hidT_ready = sem("hidT_full"), sem("hidT_ready")
        y_full, yA_ready, yB_ready = sem("y_full"), sem("yA_ready"), sem("yB_ready")
        onehot_ready, meta_full, meta_taken = sem("onehot_ready"), sem("meta_full"), sem("meta_taken")
        idx_ready = sem("idx_ready")
        T_full, TA_ready, TB_ready = sem("T_full"), sem("TA_ready"), sem("TB_ready")
        x_loaded_w, x_onehot, x_meta, x_idx, x_gathered = (sem("x_loaded_w"), sem("x_onehot"), sem("x_meta"), sem("x_idx"),
                                                           sem("x_gathered"))
        x_T, x_hgT, x_gu, x_silu, x_hid = sem("x_T"), sem("x_hgT"), sem("x_gu"), sem("x_silu"), sem("x_hid")
        x_hidT_full, x_hidT, x_y, x_y_sb, x_stored = (sem("x_hidT_full"), sem("x_hidT"), sem("x_y"), sem("x_y_sb"),
                                                      sem("x_stored"))
        x_step, x_moved = sem("x_step"), sem("x_moved")
        ws_loaded, sh_hid_ready = sem("ws_loaded"), sem("sh_hid_ready")
        sh_full, sh_taken = sem("sh_full"), sem("sh_taken")
        sum_ready, sum_stored = sem("sum_ready"), sem("sum_stored")
        all_added = sem("all_added")
        sum_loaded = [sem(f"sum_loaded{t}") for t in range(NT)]
        var2_ready, std2_ready, scale2_ready = sem("var2_ready"), sem("std2_ready"), sem("scale2_ready")
        normed2, gained2, out_ready, last_ready = sem("normed2"), sem("gained2"), sem("out_ready"), sem("last_ready")

        turns = Turns(8)
        for t in range(NT):
            turns.take(("xT", t, 0))
            turns.take(("xT", t, 1))
        turns.take("alr", 2)
        for f in range(4):
            turns.take(("qk", f), 2)
        for t in range(NT):
            turns.take(("pre", t))
        for t in range(NT - 1):
            turns.take(("va", t))
        for t in range(NT - 1):
            turns.take(("vb", t))
        turns.take(("va", NT - 1))
        turns.take(("vb", NT - 1))
        for t in range(NT):
            turns.take(("cum", t), 2)
        for f in range(4):
            turns.take(("g", f), 2)
        turns.take("ws")
        turns.take("ws_s")
        for t in range(NT):
            turns.take(("k2", t))
        turns.take(("u", 0), 2)
        for c in range(NCH):
            turns.take(("U", c))
        turns.take(("sc", 0), 2)
        for t in range(NT - 1):
            if t < 3:
                turns.take(("u", t + 1), 2)
            if t:
                turns.take(("ms", t - 1))
            turns.take(("o", t), 2)
            turns.take(("sc", t + 1), 2)
            if t == 3:
                turns.take(("mg", 0))
            if t >= 2:
                turns.take(("sgu", t - 2))
        turns.take(("ms", 3))
        turns.take(("o", 4), 2)
        turns.take(("mg", 1))
        turns.take(("sgu", 2))
        turns.take(("ms", 4))
        turns.take("Us", 4)
        for t in range(NT):
            turns.take(("m", t), 2)
            if t < 3:
                turns.take(("mg", t + 2))
            if t < 2:
                turns.take(("sgu", t + 3))
            if t:
                turns.take(("hT", t - 1, 0))
                turns.take(("hT", t - 1, 1))
            if t > 1:
                turns.take(("logits", t - 2))
        turns.take(("logits", NT - 2))
        turns.take(("sh", 0), 2)
        turns.take(("hT", NT - 1, 0))
        turns.take(("hT", NT - 1, 1))
        turns.take(("logits", NT - 1))
        turns.take(("sh", 1), 2)
        turns.take(("sh", 2), 2)
        turns.take("pos")
        turns.take("cnt")
        turns.take(("sh", 3), 2)
        LAST = list(turns.count)

        def bank(name, n=0):
            return psum[:, turns.of[name][n][0], :]

        def claim(pe, name):
            for b, turn in turns.of[name]:
                if turn > 1:
                    pe.wait_ge(bank_empty[b], turn - 1)

        def filled(ins, name, n=0):
            ins.then_inc(bank_full[turns.of[name][n][0]], 1)

        def await_full(eng, name, n=0):
            b, turn = turns.of[name][n]
            eng.wait_ge(bank_full[b], turn)

        def emptied(ins, name, n=0):
            ins.then_inc(bank_empty[turns.of[name][n][0]], 1)

        def await_emptied(eng, name, n=0):
            b, turn = turns.of[name][n]
            eng.wait_ge(bank_empty[b], turn)

        def further_slots(eng, steps, before_them):
            eng.wait_ge(route_ready, 1)
            flag = eng.value_load(crowded[0:1, 0:1], min_val=0, max_val=1)
            with eng.If(flag > 0):
                before_them()
                with eng.Fori(0, NT - 1) as b:
                    if eng.engine == mybir.EngineType.DVE:
                        steps.move(b)
                    with eng.Fori(0, NE) as e:
                        n = b * NE + e + 1
                        steps(e, n)
                        eng.wait_ge(x_stored, 16 * n)
                        eng.sem_inc(x_passed, 1)

        SMALL = 15 + DB

        block = ctx.enter_context(nc.Block())

        @block.sync
        def _(sp):
            for t in range(NT):
                src = x_prompt[0, tok(t), :] if t < NT - 1 else x_sample.rearrange("b s d -> (b s) d")
                sp.dma_start(x_sb[0:ROWS[t], t, :], src).then_inc(x_loaded[t], 16)
            w_rows = w_in[0].rearrange("(p k) n -> p k n", k=KT)
            sp.wait_ge(gate_cleared, 1)
            sp.dma_start(walr[:, :, 0:RANK], w_rows[:, :, OA:OA + RANK]).then_inc(walr_loaded, 16)
            sp.dma_start(chunk[0][:, :, 0:H * DK], w_rows[:, :, OQ:OQ + H * DK]).then_inc(q_loaded, 16)
            sp.dma_start(chunk[0][:, :, H * DK:], w_rows[:, :, OQ + H * DK:OQ + 512]).then_inc(chunk_loaded[0], 16)
            n = 0

            def small(dst, src):
                nonlocal n
                sp.dma_start(dst, src).then_inc(small_loaded, 16)
                n += 1

            for g in range(4):
                small(wa[32 * g:32 * g + RANK, :], w_a_up[0])
            small(wa[RANK:RANK + 1, :], b_a)
            sp.dma_start(chunk[1], w_rows[:, :, OV:OV + 512]).then_inc(chunk_loaded[1], 16)
            sp.dma_start(chunk[2], w_rows[:, :, OVB:OVB + 512]).then_inc(chunk_loaded[2], 16)
            with nc.allow_non_contiguous_dma(reason="per-head gains, one column a head"):
                small(gn_gla[:, :], gla_norm_g[0].rearrange("h v -> v h"))
                small(gn_gmlp[:, :], gmlp_norm_g[0].rearrange("h v -> v h"))
            small(gln_gb[:, 0, :], gmlp_ln_g[0].partition_broadcast(P))
            small(gln_gb[:, 1, :], gmlp_ln_b[0].partition_broadcast(P))
            small(ln_gb[:, 0, :], ln1_g[0].partition_broadcast(P))
            small(ln_gb[:, 1, :], ln1_b[0].partition_broadcast(P))
            small(rbias[:, :], router_bias[0].partition_broadcast(P))
            small(work[:, 0, :].rearrange("p (h s) -> p h s", h=H), w_s[0].rearrange("h t s -> t h s"))
            sp.wait_ge(first_consts, 1)
            for b in range(DB):
                small(work[b * DS:(b + 1) * DS, 1, 0:H * NS].rearrange("p (h s) -> p h s", h=H)[:, :, b * DS:(b + 1) * DS],
                      w_s[0, :, 0:DS, 0:DS].rearrange("h t s -> t h s"))
            small(bs[:, :, :], b_s[0].partition_broadcast(P))
            small(wr[:, :, :], w_router[0].rearrange("(p k) n -> p k n", k=KT))
            assert n == SMALL, n
            await_full(sp, ("qk", 3), 0)
            await_full(sp, ("qk", 3), 1)
            sp.dma_start(chunk[0], w_rows[:, :, OG:OG + 512]).then_inc(chunk_loaded[0], 16)
            await_full(sp, ("va", NT - 1))
            sp.dma_start(chunk[1], w_rows[:, :, OU:OU + 512]).then_inc(chunk_loaded[1], 16)
            wo_rows = w_out[0].rearrange("(k p) n -> p k n", p=P)
            await_full(sp, ("vb", NT - 1))
            sp.dma_start(chunk[2], wo_rows[:, :, 0:512]).then_inc(chunk_loaded[2], 16)
            await_full(sp, ("g", 3), 0)
            await_full(sp, ("g", 3), 1)
            sp.dma_start(chunk[0], wo_rows[:, :, 512:1024]).then_inc(chunk_loaded[0], 16)
            await_full(sp, ("u", 3), 0)
            await_full(sp, ("u", 3), 1)
            for r in range(PAIRS):
                sp.dma_start(S0[:, r, :, :], state_gla[0, :, 2 * r:2 * r + 2].rearrange("b h k v -> (h k) b v")).then_inc(S0_loaded, 16)
            sp.wait_ge(vg_ready, NT)
            sp.dma_start(v_sample[0].rearrange("b s n -> (b s) n"), v_b[0:NS, NT - 1, :]).then_inc(out_stored, 16)
            await_emptied(sp, ("U", NCH - 1))
            sp.dma_start(state_prompt[0, 0].rearrange("(r h) k v -> (h k) r v", h=2), S[:, NCH, :, :]).then_inc(out_stored, 16)
            await_emptied(sp, "Us", 2 * PAIRS - 1)
            for r in range(PAIRS):
                sp.dma_start(state_sample[0, :, 2 * r:2 * r + 2].rearrange("b h k v -> (h k) b v"), S0[:, r, :, :]).then_inc(out_stored, 16)
            await_full(sp, ("sgu", NT - 1))
            sp.wait_ge(out_stored, 16 * 4)
            for g, w in enumerate((ws_gate, ws_up)):
                sp.dma_start(ws_gu[:, g, :, :], w[0].rearrange("(p k) n -> p k n", k=KT)).then_inc(ws_loaded, 16)
            sp.dma_start(ws_d, ws_down[0].rearrange("(k p) n -> p k n", p=P)).then_inc(ws_loaded, 16)
            for half in range(2):
                spare = slice(N + half * NS, N + (half + 1) * NS)
                sp.dma_start(sum_dram[spare, :], x_sb[NS:P, NT - 1, :]).then_inc(spare_stored, 16)
            for t in range(NT):
                sp.wait_ge(h_ready, t + 1)
                sp.dma_start(h_dram[tok(t), :], x_sb[0:ROWS[t], t, :]).then_inc(h_stored[t], 16)
            sp.dma_start(ln_gb[:, 0, :], ln2_g[0].partition_broadcast(P)).then_inc(ln2_loaded, 16)
            sp.dma_start(ln_gb[:, 1, :], ln2_b[0].partition_broadcast(P)).then_inc(ln2_loaded, 16)

            def expert(w, e):
                return w[0, bass.ds(e, 1)].rearrange("o (p k) n -> p (o k n)", p=P)

            def load_gu(u, e):
                sp.dma_start(gu_flat(u, 0), expert(w_gate, e)).then_inc(gu_loaded[u], 16)
                sp.dma_start(gu_flat(u, 1), expert(w_up, e)).then_inc(gu_loaded[u], 16)

            def load_wd(s, e):
                sp.dma_start(wd_flat(s), expert(w_down, e)).then_inc(wd_loaded[s], 16)

            await_full(sp, ("m", NT - 1), 0)
            await_full(sp, ("m", NT - 1), 1)
            for u in range(2):
                load_gu(u, u)
                load_wd(u, u)
            for t in range(NT):
                sp.wait_ge(sum_ready, t + 1)
                sp.dma_start(sum_dram[tok(t), :], x_sb[0:ROWS[t], t, :]).then_inc(sum_stored, 16)

            await_full(sp, ("sh", 3), 0)
            await_full(sp, ("sh", 3), 1)
            for e in range(2):
                sp.wait_ge(gu_full, e + 1)
                load_gu(e, e + 2)
                load_wd(e + 2, e + 2)
            with sp.Fori(0, NE // 4 - 1) as j:
                for q in range(4):
                    sp.wait_ge(gu_full, 4 * j + (q + 3))
                    load_gu(q % 2, 4 * j + (q + 4))
                    sp.wait_ge(y_full, 8 * j + (2 * q + 2))
                    load_wd(q, 4 * j + (q + 4))

            def further(e, n):
                for g, w in enumerate((w_gate, w_up)):
                    sp.dma_start(gu_flat(1, g), expert(w, e)).then_inc(x_loaded_w, 16)
                sp.dma_start(wd_flat(1), expert(w_down, e)).then_inc(x_loaded_w, 16)

            further_slots(sp, further, lambda: sp.wait_ge(y_full, 2 * NE))
            sp.wait_ge(all_added, 1)
            for t in range(NT):
                sp.dma_start(x_sb[0:ROWS[t], t, :], sum_dram[tok(t), :]).then_inc(sum_loaded[t], 16)
            for t in range(NT):
                if t < NT - 2:
                    sp.wait_ge(out_ready, t + 1)
                else:
                    sp.wait_ge(last_ready, t - (NT - 3))
                dst = y_prompt[0, tok(t), :] if t < NT - 1 else y_sample.rearrange("b s d -> (b s) d")
                sp.dma_start(dst, x_sb[0:ROWS[t], t, :]).then_inc(out_stored, 16)
            sp.wait_ge(out_stored, 16 * (4 + NT))

        @block.gpsimd
        def _(pool):
            count = [0]

            def link(ins):
                count[0] += 1
                ins.then_inc(pool_step, 1)
                pool.wait_ge(pool_step, count[0])

            def keep(view, pattern, base, cm, op=ALU.is_ge, fill=0.0):
                link(pool.affine_select(out=view, in_=view, pattern=pattern, compare_op=op, fill=fill,
                                        base=base, channel_multiplier=cm))

            pool.memset(work[:, 1, :], 0.0)
            link(pool.memset(ident[:, :], 0.0))
            pool.affine_select(out=ident[:, :], in_=ident[:, :], pattern=[[-1, P]], compare_op=ALU.not_equal, fill=1.0,
                               base=0, channel_multiplier=1).then_inc(first_consts, 1)
            pool.memset(ones_w[:, :], 1.0)
            pool.memset(mean_w[:, :], 1.0 / P)
            pool.memset(eps5[:, :], 1e-5)
            pool.memset(eps6[:, :], 1e-6)
            pool.memset(mv[:, :, :], 1.0)
            pool.memset(mv1[:, :, :], 1.0)
            pool.memset(posm[:, :, :], 0.0)
            pool.memset(aux[:, :, :, :], 0.0)
            pool.memset(before[:, :], 1.0)
            pool.memset(upto[:, :], 1.0)
            pool.memset(cum_p[:, :, :], 1.0)
            pool.memset(cum_s[:, :, :], 1.0)
            pool.memset(mid_p[:, :], 1.0)
            pool.memset(mid_s[:, :], 1.0)
            pool.memset(tri8[:, :, :], 1.0)
            pool.memset(seq_mask[:, :], 1.0)
            link(pool.memset(scT[:, :, :, :], 0.0))
            keep(before[:, :], [[1, P]], -1, -1)
            keep(upto[:, :], [[1, P]], 0, -1)
            keep(tri8[:, :, :], [[1, NG], [-1, NG]], -1, 0)
            keep(seq_mask[:, :], [[-DS, DB]], 0, 1)
            keep(seq_mask[:, :], [[DS, DB]], DS - 1, -1)
            for cum, mid, n, c in ((cum_p, mid_p, P, CH), (cum_s, mid_s, NS, DS)):
                for kind in range(3):
                    v = cum[:, kind, :].rearrange("p (n c) -> p n c", c=c)
                    keep(v, [[-c, n // c], [0, c]], 0, 1)
                    keep(v, [[c, n // c], [0, c]], c - 1, -1)
                    if kind < 2:
                        keep(v, [[c, n // c], [1, c]], 0, -1)
                    else:
                        keep(v, [[-c, n // c], [-1, c]], -1, 1)
                v = mid[:, :].rearrange("p (n c) -> p n c", c=c)
                keep(v, [[-c, n // c], [0, c]], 0, 1)
                keep(v, [[c, n // c], [0, c]], c // 2 - 1, -1)
                link(pool.tensor_tensor(cum[:, 0, :], cum[:, 0, :], mid[:, :], ALU.subtract))
            link(pool.iota(slot10k[:, :], [[1, P]], base=int(HIT), channel_multiplier=0,
                           allow_small_or_imprecise_dtypes=True))
            link(pool.iota(part[:, :], [[0, 1]], base=0, channel_multiplier=1,
                           allow_small_or_imprecise_dtypes=True))
            for t in range(NT):
                link(pool.tensor_copy(aux[:, t, 0:NE, 0], part[:, 0:1].to_broadcast([P, NE])))
                ins = pool.memset(aux[:, t, 0:NE, 1], t * P - N)
                if t < NT - 1:
                    link(ins)
            ins.then_inc(consts_ready, 1)

            await_emptied(pool, ("k2", NT - 1))
            await_full(pool, ("u", 3), 0)
            await_full(pool, ("u", 3), 1)
            pool.tensor_tensor(k2m, k2[0:NS, NT - 1, :].unsqueeze(1).to_broadcast([NS, DB, H * DK]),
                               seq_mask[:, :].unsqueeze(2).to_broadcast([NS, DB, H * DK]), ALU.mult).then_inc(k2m_ready, 1)

            for t in range(NT):
                r = ROWS[t]
                pool.wait_ge(h_stored[t], 16)
                await_full(pool, ("hT", t, 0))
                await_full(pool, ("hT", t, 1))
                link(pool.tensor_scalar(x_sb[0:r, t, :], x_sb[0:r, t, :], ALPHA, None, ALU.mult))
            link(pool.memset(hg[:, :, :], 0.0))
            for f in range(FK):
                for g in (f, FK + f):
                    await_emptied(pool, ("sh", g), 0)
                    await_emptied(pool, ("sh", g), 1)
                pool.tensor_tensor(sh_hid[:, f, :], sh_hid[:, f, :], sh_silu[:, f, :], ALU.mult).then_inc(sh_hid_ready, 1)
            pool.wait_ge(route_ready, 1)
            pool.wait_ge(spare_stored, 16 * 2)

            last_token, last_row = pool.to_reg(N - 1), pool.to_reg(N + P - 1)

            def gather(u, n):
                pool.wait_ge(idx_ready, n)
                pool.sem_inc(pool_passed, 1)
                pool.indirect_dma_start(hg[:, u, :], None, h_dram,
                                        bass.IndirectOffsetOnAxis(ap=idx[:, u:u + 1], axis=0),
                                        bounds_check=last_token, oob_is_err=False).then_inc(gathered[u], 16)

            def add_rows(u, n):
                pool.wait_ge(yA_ready, n)
                pool.wait_ge(yB_ready, n)
                if not (isinstance(n, int) and n == 1):
                    pool.wait_ge(added, 16 * (n - 1))
                pool.sem_inc(pool_passed, 1)
                pool.indirect_dma_start(sum_dram, bass.IndirectOffsetOnAxis(ap=yrow[:, u:u + 1], axis=0),
                                        y_sb[:, u, :], None, bounds_check=last_row,
                                        oob_is_err=True, compute_op=ALU.add).then_inc(added, 16)

            def add_shared(t):
                r = ROWS[t]
                pool.wait_ge(sh_taken, t + 1)
                pool.tensor_tensor(x_sb[0:r, t, :], x_sb[0:r, t, :], sh_rows(t)[0:r, :], ALU.add).then_inc(sum_ready, 1)

            gather(0, 1)
            gather(1, 2)
            add_shared(0)
            add_shared(1)
            pool.wait_ge(T_full, 2)
            gather(0, 3)
            for t in range(2, NT):
                add_shared(t)
            pool.wait_ge(sum_stored, 16 * NT)
            pool.wait_ge(T_full, 4)
            gather(1, 4)
            add_rows(0, 1)
            pool.wait_ge(T_full, 6)
            gather(0, 5)
            add_rows(1, 2)
            with pool.Fori(1, NE // 2 - 2) as j:
                for u in range(2):
                    pool.wait_ge(T_full, 4 * j + 2 * u + 4)
                    gather((u + 1) % 2, 2 * j + (u + 4))
                    add_rows(u, 2 * j + (u + 1))
            for i in range(NE - 4, NE):
                if i + 3 < NE:
                    pool.wait_ge(T_full, 2 * (i + 2))
                    gather((i + 1) % 2, i + 4)
                add_rows(i % 2, i + 1)
            pool.wait_ge(added, 16 * NE)

            def further(e, n):
                pool.wait_ge(x_idx, n)
                pool.sem_inc(pool_passed, 1)
                pool.indirect_dma_start(hg[:, 0, :], None, h_dram, bass.IndirectOffsetOnAxis(ap=idx[:, 0:1], axis=0),
                                        bounds_check=last_token, oob_is_err=False).then_inc(x_gathered, 16)
                pool.wait_ge(x_y_sb, n)
                pool.sem_inc(pool_passed, 1)
                pool.indirect_dma_start(sum_dram, bass.IndirectOffsetOnAxis(ap=idx[:, 0:1], axis=0), y_sb[:, 0, :], None,
                                        bounds_check=last_row, oob_is_err=True, compute_op=ALU.add).then_inc(x_stored, 16)

            further_slots(pool, further, lambda: None)
            pool.sem_inc(all_added, 1)
            for t in range(NT - 2):
                r = ROWS[t]
                pool.wait_ge(gained2, t + 1)
                pool.tensor_tensor(x_sb[0:r, t, :], x_sb[0:r, t, :], ln_gb[0:r, 1, :], ALU.add).then_inc(out_ready, 1)

        @block.tensor
        def _(pe):
            pe.wait_ge(first_consts, 1)

            def transposes(name, src, t):
                r = ROWS[t]
                for h in range(2):
                    claim(pe, (name, t, h))
                    for k in range(4):
                        ins = pe.transpose(bank((name, t, h))[:, k * P:k * P + r], src[0:r, t, 4 * h + k::KT], ident[0:r, 0:r])
                    filled(ins, (name, t, h))

            for t in range(NT):
                pe.wait_ge(x_loaded[t], 16)
                transposes("xT", x_sb, t)
            for t in range(NT):
                await_emptied(pe, ("xT", t, 0))
                await_emptied(pe, ("xT", t, 1))

            def feature_rows(name, w):
                claim(pe, name)
                for k in range(KT):
                    for n in range(2):
                        ins = pe.matmul(bank(name, n)[:, 0:NH], w(k), xT[:, k, HALVES[n]], start=(k == 0), stop=(k == KT - 1))
                        if k == KT - 1:
                            filled(ins, name, n)

            def token_rows(name, t, c):
                claim(pe, (name, t))
                for k in range(KT):
                    ins = pe.matmul(bank((name, t)), xT[:, k, tok(t)], chunk[c][:, k, :], start=(k == 0), stop=(k == KT - 1))
                filled(ins, (name, t))

            def sample_rows(outs, rows, ws):
                for k in range(KT):
                    for half, (name, n) in enumerate(outs):
                        ins = pe.matmul(bank(name, n)[half * NS:(half + 1) * NS, :], rows[:, k, SEQ:N], ws[half][:, k, :],
                                        start=(k == 0), stop=(k == KT - 1))
                        if k == KT - 1:
                            filled(ins, name, n)

            pe.wait_ge(walr_loaded, 16)
            claim(pe, "alr")
            for k in range(KT // 4):
                for n in range(2):
                    for g in range(4):
                        ins = pe.matmul(bank("alr", n)[32 * g:32 * g + 32, 0:NH], walr[:, 2 * g + k, :], xT[:, 2 * g + k, HALVES[n]],
                                        start=(k == 0), stop=(k == KT // 4 - 1))
                    if k == KT // 4 - 1:
                        filled(ins, "alr", n)
            pe.wait_ge(q_loaded, 16)
            for f in range(4):
                if f == PAIRS:
                    pe.wait_ge(chunk_loaded[0], 16)
                feature_rows(("qk", f), lambda k, f=f: chunk[0][:, k, f * P:(f + 1) * P])
            await_emptied(pe, "alr", 0)
            await_emptied(pe, "alr", 1)
            pe.wait_ge(small_loaded, 16 * SMALL)
            for t in range(NT):
                claim(pe, ("pre", t))
                filled(pe.matmul(bank(("pre", t))[0:ROWS[t], 0:H * DK], alrT[:, tok(t)], wa[:, :], start=True, stop=True), ("pre", t))
            pe.wait_ge(chunk_loaded[1], 16)
            for t in range(NT - 1):
                token_rows("va", t, 1)
            pe.wait_ge(chunk_loaded[2], 16)
            for t in range(NT - 1):
                token_rows("vb", t, 2)
            claim(pe, ("va", NT - 1))
            claim(pe, ("vb", NT - 1))
            sample_rows(((("va", NT - 1), 0), (("vb", NT - 1), 0)), xT, (chunk[1], chunk[2]))
            pe.wait_ge(la_ready, 2)
            pe.wait_ge(consts_ready, 1)
            for t in range(NT):
                r = ROWS[t]
                cum = cum_p if t < NT - 1 else cum_s
                claim(pe, ("cum", t))
                for p in range(PAIRS):
                    filled(pe.matmul(bank(("cum", t), p)[:, 0:3 * r], la[0:r, t, p * P:(p + 1) * P],
                                     cum[:, :, :].rearrange("p k n -> p (k n)"), start=True, stop=True), ("cum", t), p)
            pe.wait_ge(chunk_loaded[0], 32)
            for f in range(4):
                feature_rows(("g", f), lambda k, f=f: chunk[0][:, k, f * P:(f + 1) * P])

            def u_rows(f):
                feature_rows(("u", f), lambda k: chunk[1][:, k, f * P:(f + 1) * P])

            claim(pe, "ws")
            for h in range(H):
                ins = pe.transpose(bank("ws")[:, h * P:(h + 1) * P], work[:, 0, h * P:(h + 1) * P], ident[:, :])
            filled(ins, "ws")
            claim(pe, "ws_s")
            for h in range(H):
                ins = pe.transpose(bank("ws_s")[0:NS, h * NS:(h + 1) * NS], work[0:NS, 1, h * NS:(h + 1) * NS], ident[0:NS, 0:NS])
            filled(ins, "ws_s")

            for t in range(NT):
                pe.wait_ge(qk_ready, PAIRS * (t + 1))
                claim(pe, ("k2", t))
                for p in range(PAIRS):
                    ins = pe.transpose(bank(("k2", t))[0:ROWS[t], p * P:(p + 1) * P], E[:, t, p, 3, 0:ROWS[t]], ident[:, :])
                filled(ins, ("k2", t))
            pe.wait_ge(chunk_loaded[1], 32)
            u_rows(0)
            for t in range(NT):
                await_emptied(pe, ("va", t))
            for c in range(NCH):
                t, lo = c // 2, CH * (c % 2)
                await_emptied(pe, ("k2", t))
                claim(pe, ("U", c))
                for h in range(H):
                    ins = pe.matmul(bank(("U", c))[DK * (h % 2):DK * (h % 2) + DK, (h // 2) * DV:(h // 2 + 1) * DV],
                                    k2[lo:lo + CH, t, h * DK:(h + 1) * DK], v_a[lo:lo + CH, t, h * DV:(h + 1) * DV],
                                    start=True, stop=True)
                filled(ins, ("U", c))

            def scores(t):
                r = ROWS[t]
                claim(pe, ("sc", t))
                for h in range(H):
                    q = slice(DK * (h % 2), DK * (h % 2) + DK)
                    ins = pe.matmul(bank(("sc", t), h % 2)[0:r, h // 2 * P:h // 2 * P + r], E[q, t, h // 2, 2, 0:r],
                                    E[q, t, h // 2, 0, 0:r], start=True, stop=True)
                    if h > 1:
                        filled(ins, ("sc", t), h % 2)

            def gla_rows(t):
                r = ROWS[t]
                if t < NT - 1:
                    await_emptied(pe, ("U", 2 * t))
                else:
                    pe.wait_ge(S0_loaded, 16 * PAIRS)
                await_emptied(pe, ("sc", t), 0)
                await_emptied(pe, ("sc", t), 1)
                claim(pe, ("o", t))
                def out(h):
                    return bank(("o", t), h % 2)[:, h // 2 * P:h // 2 * P + r]

                if t < NT - 1:
                    parts = [(slice(c * CH, (c + 1) * CH), 2 * t + c) for c in range(2) if 2 * t + c > 0]
                else:
                    parts = [(slice(b * DS, (b + 1) * DS), b) for b in range(DB)]
                for pair in range(PAIRS):
                    heads = (2 * pair, 2 * pair + 1)
                    for h in heads:
                        pe.matmul(out(h), v_a[:, t, h * DV:(h + 1) * DV], scT[:, t % 2, h, 0:r], start=True, stop=True,
                                  skip_group_check=True)
                    for cols, n in parts:
                        for h in heads:
                            q = slice(DK * (h % 2), DK * (h % 2) + DK)
                            state = S[q, n, pair, :] if t < NT - 1 else S0[q, pair, n, :]
                            ins = pe.matmul(out(h)[:, cols], state, E[q, t, pair, 1, cols], start=False, stop=True,
                                            skip_group_check=True)
                            if pair == PAIRS - 1 and n == parts[-1][1]:
                                filled(ins, ("o", t), h % 2)

            def mean_square(name, t, squared, n):
                pe.wait_ge(squared, n * (t + 1))
                claim(pe, (name, t))
                filled(pe.matmul(bank((name, t))[:, 0:H * ROWS[t]], mean_w[:, :], work[:, 0 if name == "ms" else 1, 0:H * ROWS[t]],
                                 start=True, stop=True), (name, t))

            def gated_rows(t):
                r = ROWS[t]
                w = wsT if t < NT - 1 else wsT_s
                pe.wait_ge(vg_ready, t + 1)
                await_emptied(pe, "ws")
                await_emptied(pe, "ws_s")
                claim(pe, ("sgu", t))
                for h in range(H):
                    ins = pe.matmul(bank(("sgu", t))[:, h * r:(h + 1) * r], v_b[0:r, t, h * P:(h + 1) * P], w[:, h, :],
                                    start=True, stop=True)
                filled(ins, ("sgu", t))

            scores(0)
            for t in range(NT - 1):
                if t < 3:
                    u_rows(t + 1)
                if t:
                    mean_square("ms", t - 1, sq_gla, 2)
                gla_rows(t)
                scores(t + 1)
                if t == 3:
                    mean_square("mg", 0, sq_gmlp, 1)
                if t >= 2:
                    gated_rows(t - 2)
            mean_square("ms", 3, sq_gla, 2)
            gla_rows(4)
            mean_square("mg", 1, sq_gmlp, 1)
            gated_rows(2)
            mean_square("ms", 4, sq_gla, 2)
            pe.wait_ge(k2m_ready, 1)
            claim(pe, "Us")
            for p in range(PAIRS):
                for b in range(DB):
                    for hh in range(2):
                        h = 2 * p + hh
                        ins = pe.matmul(bank("Us", 2 * p + b // 4)[DK * hh:DK * hh + DK, (b % 4) * DV:(b % 4 + 1) * DV],
                                        k2m[:, b, h * DK:(h + 1) * DK], v_a[0:NS, NT - 1, h * DV:(h + 1) * DV],
                                        start=True, stop=True)
                    if b % 4 == 3:
                        filled(ins, "Us", 2 * p + b // 4)

            def out_rows(t):
                pe.wait_ge(gla_ready, t + 1)
                pe.wait_ge(gmlp_ready, t + 1)
                claim(pe, ("m", t))
                if t == NT - 1:
                    sample_rows(((("m", t), 0), (("m", t), 1)), merged, (chunk[2], chunk[0]))
                    return
                for n in range(2):
                    w = chunk[2] if n == 0 else chunk[0]
                    for k in range(KT):
                        ins = pe.matmul(bank(("m", t), n), merged[:, k, tok(t)], w[:, k, :],
                                        start=(k == 0), stop=(k == KT - 1))
                    filled(ins, ("m", t), n)

            def turn_h(t):
                pe.wait_ge(h_ready, t + 1)
                transposes("hT", x_sb, t)

            def router(t):
                await_emptied(pe, ("hT", t, 0))
                await_emptied(pe, ("hT", t, 1))
                claim(pe, ("logits", t))
                for k in range(KT):
                    ins = pe.matmul(bank(("logits", t))[0:ROWS[t], 0:NE], xT[:, k, tok(t)], wr[:, k, :],
                                    start=(k == 0), stop=(k == KT - 1))
                filled(ins, ("logits", t))

            def shared_features(f):
                feature_rows(("sh", f), lambda k: ws_gu[:, f // FK, k, f % FK * P:(f % FK + 1) * P])

            pe.wait_ge(chunk_loaded[2], 32)
            pe.wait_ge(chunk_loaded[0], 48)
            for t in range(NT):
                out_rows(t)
                if t < 3:
                    mean_square("mg", t + 2, sq_gmlp, 1)
                if t < 2:
                    gated_rows(t + 3)
                if t:
                    turn_h(t - 1)
                if t > 1:
                    router(t - 2)
            router(NT - 2)
            pe.wait_ge(ws_loaded, 48)
            claim(pe, ("sh", 0))
            for k in range(KT):
                ins = pe.matmul(bank(("sh", 0), 0)[:, 0:NH], ws_gu[:, 0, k, 0:P], xT[:, k, HALVES[0]], start=(k == 0), stop=(k == KT - 1))
            filled(ins, ("sh", 0), 0)
            turn_h(NT - 1)
            router(NT - 1)
            for k in range(KT):
                ins = pe.matmul(bank(("sh", 0), 1)[:, 0:NH], ws_gu[:, 0, k, 0:P], xT[:, k, HALVES[1]], start=(k == 0), stop=(k == KT - 1))
            filled(ins, ("sh", 0), 1)
            shared_features(1)
            shared_features(2)
            mask = scratch(1, NT * NE).rearrange("p (t e) -> p t e", t=NT)
            pe.wait_ge(mask_ready, 1)
            claim(pe, "pos")
            for t in range(NT):
                ins = pe.matmul(bank("pos")[:, t * NE:(t + 1) * NE], before[:, :], mask[:, t, :], start=True, stop=(t == 0))
                for s in range(t):
                    ins = pe.matmul(bank("pos")[:, t * NE:(t + 1) * NE], ones_w[:, :], mask[:, s, :], start=False, stop=(s == t - 1))
            filled(ins, "pos")
            claim(pe, "cnt")
            for t in range(NT):
                ins = pe.matmul(bank("cnt")[:, 0:NE], ones_w[:, :], mask[:, t, :], start=(t == 0), stop=(t == NT - 1))
            filled(ins, "cnt")
            shared_features(3)
            for b in range(8):
                pe.wait_ge(bank_empty[b], LAST[b])

            def gate_up(u, loads):
                pe.wait_ge(gu_loaded[u], loads)
                for k in range(KT):
                    ins = pe.matmul(psum[:, u, :], hgT[:, u, k * P:(k + 1) * P], gu_w(u)[:, :, k, :], start=(k == 0), stop=(k == KT - 1))
                ins.then_inc(gu_full, 1)

            def hid_transpose(u, rows):
                for k in range(FK):
                    ins = pe.transpose(psum[:, 6, k * P:k * P + rows], hid[0:rows, u, k::FK], ident[0:rows, 0:rows])
                ins.then_inc(hidT_full, 1)

            def down(u, s, rows):
                for n in range(2):
                    for k in range(FK):
                        ins = pe.matmul(psum[0:rows, 4 + n, :], hidT[:, u, k * P:k * P + rows], wd_w(s)[:, k, n * 512:(n + 1) * 512],
                                        start=(k == 0), stop=(k == FK - 1))
                    ins.then_inc(y_full, 1)

            def tell(u, e):
                for t in range(NT):
                    ins = pe.matmul(psum[:, 7, 0:MC], onehot[:, u, t, :], aux[:, t, bass.ds(e, 1), :].rearrange("p o c -> p (o c)"),
                                    start=(t == 0), stop=(t == NT - 1))
                ins.then_inc(meta_full, 1)

            def turn_rows(u):
                for h in range(2):
                    for k in range(4):
                        ins = pe.transpose(psum[:, 2 + h, k * P:(k + 1) * P], hg[:, u, 4 * h + k::KT], ident[:, :])
                    ins.then_inc(T_full, 1)

            def first_tell(e):
                pe.wait_ge(onehot_ready, e + 1)
                if e:
                    pe.wait_ge(meta_taken, e)
                tell(e % 2, e)

            def shared_down(t):
                r = ROWS[t]
                if t > 1:
                    pe.wait_ge(sh_taken, t - 1)
                for n in range(2):
                    for k in range(FK):
                        ins = pe.matmul(psum[0:r, 4 - t % 2 * 4 + n, :], sh_hid[:, k, tok(t)], ws_d[:, k, n * 512:(n + 1) * 512],
                                        start=(k == 0), stop=(k == FK - 1))
                ins.then_inc(sh_full, 1)

            first_tell(0)
            first_tell(1)
            pe.wait_ge(sh_hid_ready, FK)
            shared_down(0)
            shared_down(1)
            pe.wait_ge(gathered[0], 16)
            turn_rows(0)
            first_tell(2)
            shared_down(2)
            pe.wait_ge(gathered[1], 16)
            pe.wait_ge(TA_ready, 1)
            pe.wait_ge(TB_ready, 1)
            turn_rows(1)
            shared_down(3)
            first_tell(3)
            shared_down(4)
            pe.wait_ge(sh_taken, 4)
            gate_up(0, 32)

            def expert_steps(q, j):
                i, u = 4 * j + q, q % 2
                first = isinstance(j, int) and i == 0
                half = 2 * j + q // 2
                left = NE - i if isinstance(j, int) else NE
                pe.wait_ge(hid_ready, i + 1)
                if not first:
                    pe.wait_ge(hidT_ready, i)
                hid_transpose(u, P)
                if left > 1:
                    pe.wait_ge(TA_ready, i + 2)
                    pe.wait_ge(TB_ready, i + 2)
                    gate_up(1 - u, 32 * (half + (1 + u)))
                if left > AHEAD:
                    pe.wait_ge(onehot_ready, i + AHEAD + 1)
                    pe.wait_ge(meta_taken, i + AHEAD)
                    tell(u, i + AHEAD)
                if left > 2:
                    pe.wait_ge(gathered[u], 16 * (half + 2))
                    turn_rows(u)
                pe.wait_ge(hidT_ready, i + 1)
                pe.wait_ge(wd_loaded[q], 16 * (j + 1))
                if not first:
                    pe.wait_ge(yA_ready, i)
                    pe.wait_ge(yB_ready, i)
                else:
                    pe.wait_ge(sh_taken, NT)
                down(u, q, P)

            for q in range(4):
                expert_steps(q, 0)
            with pe.Fori(1, NE // 4 - 1) as j:
                for q in range(4):
                    expert_steps(q, j)
            for q in range(4):
                expert_steps(q, NE // 4 - 1)

            def further(e, n):
                pe.wait_ge(x_onehot, n)
                for t in range(NT):
                    ins = pe.matmul(psum[:, 7, 0:MC], onehot[:, 0, t, :], aux[:, t, bass.ds(e, 1), :].rearrange("p o c -> p (o c)"),
                                    start=(t == 0), stop=(t == NT - 1))
                ins.then_inc(x_meta, 1)
                pe.wait_ge(x_gathered, 16 * n)
                for k in range(KT):
                    ins = pe.transpose(psum[:, 2 + k // 4, k % 4 * P:(k % 4 + 1) * P], hg[:, 0, k::KT], ident[:, :])
                ins.then_inc(x_T, 1)
                pe.wait_ge(x_hgT, n)
                pe.wait_ge(x_loaded_w, 48 * n)
                for k in range(KT):
                    ins = pe.matmul(psum[:, 0, :], hgT[:, 0, k * P:(k + 1) * P], gu_w(1)[:, :, k, :], start=(k == 0), stop=(k == KT - 1))
                ins.then_inc(x_gu, 1)
                pe.wait_ge(x_hid, n)
                for k in range(FK):
                    ins = pe.transpose(psum[:, 6, k * P:(k + 1) * P], hid[:, 0, k::FK], ident[:, :])
                ins.then_inc(x_hidT_full, 1)
                pe.wait_ge(x_hidT, n)
                for c in range(2):
                    for k in range(FK):
                        ins = pe.matmul(psum[:, 4 + c, :], hidT[:, 0, k * P:(k + 1) * P], wd_w(1)[:, k, c * 512:(c + 1) * 512],
                                        start=(k == 0), stop=(k == FK - 1))
                ins.then_inc(x_y, 1)

            def banks_read():
                pe.wait_ge(yA_ready, NE)
                pe.wait_ge(yB_ready, NE)

            further_slots(pe, further, banks_read)

        @block.scalar
        def _(act):
            count = [0]

            def link(ins):
                count[0] += 1
                ins.then_inc(act_step, 1)
                act.wait_ge(act_step, count[0])

            def heads(view, r):
                return view.rearrange("p (h n) -> p h n", h=4)[:, :, 0:r]

            for t in range(NT):
                await_full(act, ("xT", t, 0))
                emptied(act.activation(xT[:, 0:4, tok(t)], heads(bank(("xT", t, 0)), ROWS[t]), ACT.Copy), ("xT", t, 0))

            def features(name, out, func):
                for n in range(2):
                    await_full(act, name, n)
                    emptied(act.activation(out[:, HALVES[n]], bank(name, n)[:, 0:NH], func), name, n)

            for f in (2, 3):
                features(("qk", f), qkT[:, f, :], ACT.Copy)
            act.wait_ge(consts_ready, 1)
            for n, (r, cols) in enumerate(((P, slice(0, (NT - 1) * 256)), (NS, slice((NT - 1) * 256, NT * 256)))):
                tmp = arena[0:r, cols]
                act.wait_ge(negabs_ready, n + 1)
                link(act.activation(tmp, tmp, ACT.Exp))
                act.activation(tmp, tmp, ACT.Ln, bias=ones_w[0:r, 0:1]).then_inc(softplus_ready, 1)
            for t in range(NT):
                await_full(act, ("vb", t))
                emptied(act.activation(v_b[0:ROWS[t], t, :], bank(("vb", t))[P - ROWS[t]:P, :], ACT.Gelu_apprx_tanh), ("vb", t))
            for t in range(NT):
                r = ROWS[t]
                for p in range(PAIRS):
                    c = bank(("cum", t), p)[:, 0:3 * r].rearrange("p (k n) -> p k n", k=3)
                    await_full(act, ("cum", t), p)
                    act.activation(E[:, t, p, 0:2, 0:r], c[:, 0:2, :], ACT.Exp, scale=1.0 / 16)
                    act.activation(E[:, t, p, 2, 0:r], c[:, 0, :], ACT.Exp, scale=-1.0 / 16)
                    emptied(act.activation(E[:, t, p, 3, 0:r], c[:, 2, :], ACT.Exp, scale=1.0 / 16), ("cum", t), p)
            act.wait_ge(vb_var, 1)
            act.activation(rstd[:, :], mv[:, :, 1], ACT.Sqrt, bias=eps5[:, 0:1]).then_inc(vb_std, 1)
            for f in range(4):
                features(("g", f), merged[:, f, :], ACT.Silu)
            for t in range(NT):
                await_full(act, ("k2", t))
                emptied(act.activation(k2[0:ROWS[t], t, :], bank(("k2", t))[0:ROWS[t], 0:256], ACT.Copy), ("k2", t))

            def u_gelu(f):
                features(("u", f), merged[:, 4 + f, :], ACT.Gelu_apprx_tanh)

            def root(name, t, used):
                w = 4 * ROWS[t]
                await_full(act, (name, t))
                if t:
                    act.wait_ge(used, t)
                emptied(act.activation(work[:, 2 if name == "ms" else 3, 0:w], bank((name, t))[:, 0:w], ACT.Sqrt, bias=eps6[:, 0:1]), (name, t))

            def gla_squares(t):
                r = ROWS[t]
                for odd in range(2):
                    await_full(act, ("o", t), odd)
                    act.activation(work[:, 0, 0:4 * r].rearrange("p (h n) -> p h n", h=4)[:, odd::2, :],
                                   heads(bank(("o", t), odd), r)[:, 0:2, :], ACT.Square).then_inc(sq_gla, 1)

            def gmlp_squares(t):
                act.wait_ge(u_gated, t + 1)
                act.activation(work[:, 1, 0:4 * ROWS[t]].rearrange("p (h n) -> p h n", h=4), merged[:, 4:8, tok(t)],
                               ACT.Square).then_inc(sq_gmlp, 1)

            def norm_root(t):
                act.wait_ge(var1_ready, t + 1)
                act.activation(rstd1[0:ROWS[t], t:t + 1], mv1[0:ROWS[t], t, 1:2], ACT.Sqrt,
                               bias=eps5[0:ROWS[t], 0:1]).then_inc(std1_ready, 1)

            s = scratch(0, NT * NE)

            def turned_half(t):
                await_full(act, ("hT", t, 0))
                emptied(act.activation(xT[:, 0:4, tok(t)], heads(bank(("hT", t, 0)), ROWS[t]), ACT.Copy), ("hT", t, 0))

            def router(t):
                await_full(act, ("logits", t))
                emptied(act.activation(s[0:ROWS[t], t * NE:(t + 1) * NE], bank(("logits", t))[0:ROWS[t], 0:NE], ACT.Sigmoid), ("logits", t))

            u_gelu(0)
            for t in range(NT - 1):
                if t < 3:
                    u_gelu(t + 1)
                if t:
                    root("ms", t - 1, gla_ready)
                gla_squares(t)
                if t == 3:
                    root("mg", 0, gmlp_ready)
                if t >= 2:
                    gmlp_squares(t - 2)
            root("ms", 3, gla_ready)
            gla_squares(4)
            root("mg", 1, gmlp_ready)
            gmlp_squares(2)
            root("ms", 4, gla_ready)
            for t in range(NT):
                if t < 3:
                    root("mg", t + 2, gmlp_ready)
                if t < 2:
                    gmlp_squares(t + 3)
                if t:
                    turned_half(t - 1)
                norm_root(t)
                if t > 1:
                    router(t - 2)
            router(NT - 2)
            await_full(act, ("sh", 0), 0)
            emptied(act.activation(sh_silu[:, 0, HALVES[0]], bank(("sh", 0), 0)[:, 0:NH], ACT.Silu), ("sh", 0), 0)
            turned_half(NT - 1)
            router(NT - 1)
            await_full(act, ("sh", 0), 1)
            emptied(act.activation(sh_silu[:, 0, HALVES[1]], bank(("sh", 0), 1)[:, 0:NH], ACT.Silu), ("sh", 0), 1)
            features(("sh", 1), sh_silu[:, 1, :], ACT.Silu)
            features(("sh", 2), sh_hid[:, 0, :], ACT.Copy)
            features(("sh", 3), sh_hid[:, 1, :], ACT.Copy)

            def silu(u, n, rows=P):
                act.wait_ge(gu_full, n)
                act.activation(sg[0:rows, u, :], psum[0:rows, u, 0:FE], ACT.Silu).then_inc(silu_ready, 1)

            def rows_half(u, n):
                act.wait_ge(T_full, n)
                act.activation(hgT[:, u, 0:512], psum[:, 2, :], ACT.Copy).then_inc(TA_ready, 1)

            def shared_rows(t):
                r = ROWS[t]
                act.wait_ge(sh_full, t + 1)
                b = 4 - t % 2 * 4
                act.activation(sh_rows(t)[0:r, :], psum[0:r, b:b + 2, :].rearrange("p b n -> p (b n)"), ACT.Copy).then_inc(sh_taken, 1)

            shared_rows(0)
            shared_rows(1)
            rows_half(0, 1)
            shared_rows(2)
            rows_half(1, 3)
            shared_rows(3)
            shared_rows(4)
            silu(0, 1)

            def expert_steps(u, j):
                i = 2 * j + u
                left = NE - i if isinstance(j, int) else NE
                if left > 1:
                    silu(1 - u, i + 2)
                if left > 2:
                    rows_half(u, 2 * i + 5)
                if not (isinstance(j, int) and j == 0):
                    act.wait_ge(added, 16 * (i - 1))
                act.wait_ge(y_full, 2 * i + 1)
                act.activation(y_sb[:, u, 0:512], psum[:, 4, :], ACT.Copy).then_inc(yA_ready, 1)

            expert_steps(0, 0)
            expert_steps(1, 0)
            with act.Fori(1, NE // 2 - 1) as j:
                expert_steps(0, j)
                expert_steps(1, j)
            expert_steps(0, NE // 2 - 1)
            expert_steps(1, NE // 2 - 1)

            def further(e, n):
                act.wait_ge(x_T, n)
                act.activation(hgT[:, 0, :], psum[:, 2:4, :].rearrange("p b n -> p (b n)"), ACT.Copy).then_inc(x_hgT, 1)
                act.wait_ge(x_gu, n)
                act.activation(sg[:, 0, :], psum[:, 0, 0:FE], ACT.Silu).then_inc(x_silu, 1)
                act.wait_ge(x_y, n)
                act.activation(y_sb[:, 0, :], psum[:, 4:6, :].rearrange("p b n -> p (b n)"), ACT.Copy).then_inc(x_y_sb, 1)

            further_slots(act, further, lambda: act.wait_ge(added, 16 * NE))
            def root2(t):
                act.wait_ge(var2_ready, t + 1)
                act.activation(rstd1[0:ROWS[t], t:t + 1], mv1[0:ROWS[t], t, 1:2], ACT.Sqrt,
                               bias=eps5[0:ROWS[t], 0:1]).then_inc(std2_ready, 1)

            root2(0)
            for t in range(NT):
                r = ROWS[t]
                if t + 1 < NT:
                    root2(t + 1)
                act.wait_ge(scale2_ready, t + 1)
                act.activation(x_sb[0:r, t, :], x_sb[0:r, t, :], ACT.Identity, scale=rstd1[0:r, t:t + 1],
                               bias=mv1[0:r, t, 0:1]).then_inc(normed2, 1)

        @block.vector
        def _(dve):
            count = [0]

            def link(ins):
                count[0] += 1
                ins.then_inc(dve_step, 1)
                dve.wait_ge(dve_step, count[0])

            def heads(view, r):
                return view.rearrange("p (h n) -> p h n", h=4)[:, :, 0:r]

            dve.memset(wa[:, :], 0.0)
            dve.memset(walr[:, :, :], 0.0).then_inc(gate_cleared, 1)
            dve.memset(x_sb[NS:P, NT - 1, :], 0.0)
            link(dve.memset(v_a[NS:P, NT - 1, :], 0.0))
            dve.wait_ge(first_consts, 1)
            for t in range(NT):
                await_full(dve, ("xT", t, 1))
                emptied(dve.tensor_copy(xT[:, 4:8, tok(t)], heads(bank(("xT", t, 1)), ROWS[t])), ("xT", t, 1))
            for n in range(2):
                await_full(dve, "alr", n)
                emptied(dve.tensor_scalar(alrT[:, HALVES[n]], bank("alr", n)[:, 0:NH], ident[:, RANK:RANK + 1], None, ALU.add), "alr", n)
            for f in (0, 1):
                for n in range(2):
                    await_full(dve, ("qk", f), n)
                    emptied(dve.tensor_scalar(qkT[:, f, HALVES[n]], bank(("qk", f), n)[:, 0:NH], DK ** -0.5, None, ALU.mult), ("qk", f), n)
            for t in range(NT):
                await_full(dve, ("pre", t))
                emptied(dve.tensor_copy(la[0:ROWS[t], t, :], bank(("pre", t))[0:ROWS[t], 0:256]), ("pre", t))
            await_emptied(dve, ("pre", NT - 1))
            await_emptied(dve, ("pre", NT - 2))
            parts = ((P, slice(0, (NT - 1) * 256)), (NS, slice((NT - 1) * 256, NT * 256)))
            laf = arena[:, 12544:13824]
            for r, cols in parts:
                dve.scalar_tensor_tensor(out=arena[0:r, cols], in0=laf[0:r, cols], scalar=-1.0, in1=laf[0:r, cols],
                                         op0=ALU.mult, op1=ALU.min).then_inc(negabs_ready, 1)
            for n, (r, cols) in enumerate(parts):
                dve.wait_ge(softplus_ready, n + 1)
                dve.scalar_tensor_tensor(out=laf[0:r, cols], in0=laf[0:r, cols], scalar=0.0, in1=arena[0:r, cols],
                                         op0=ALU.min, op1=ALU.subtract).then_inc(la_ready, 1)
            def va_rows(t):
                await_full(dve, ("va", t))
                emptied(dve.tensor_copy(v_a[0:ROWS[t], t, :], bank(("va", t))[0:ROWS[t], :]), ("va", t))

            for t in range(NT - 1):
                va_rows(t)
            dve.wait_ge(consts_ready, 1)
            for t in range(NT):
                r = ROWS[t]
                if t == NT - 1:
                    va_rows(t)
                await_emptied(dve, ("vb", t))
                link(dve.bn_stats(stats[0:r, 0, :], v_b[0:r, t, :]))
                ins = dve.bn_aggr(mv[0:r, t, :], stats[0:r, 0, :])
                link(ins) if t < NT - 1 else ins.then_inc(vb_var, 1)
            dve.wait_ge(small_loaded, 16 * SMALL)
            for t in range(NT):
                r = ROWS[t]
                await_emptied(dve, ("cum", t), 0)
                await_emptied(dve, ("cum", t), 1)
                if t < NT - 1:
                    link(dve.tensor_copy(ebl[:, :, 2 * t:2 * t + 2], E[:, t, :, 1, CH - 1::CH]))
                else:
                    link(dve.tensor_copy(ebl_s[:, :, :], E[:, t, :, 1, DS - 1:NS:DS]))
                for p in range(PAIRS):
                    for kind, f in ((0, p), (2, 2 + p)):
                        e = E[:, t, p, kind:kind + 2, 0:r]
                        if (kind, f) == (2, 2 + p):
                            await_emptied(dve, ("qk", f), 0)
                            await_emptied(dve, ("qk", f), 1)
                        ins = dve.scalar_tensor_tensor(out=e, in0=e, scalar=1e30, in1=qkT[:, f, tok(t)].unsqueeze(1).to_broadcast([P, 2, r]),
                                                       op0=ALU.min, op1=ALU.mult)
                    ins.then_inc(qk_ready, 1)
            dve.wait_ge(vb_std, 1)
            link(dve.reciprocal(rstd[:, :], rstd[:, :]))
            for t in range(NT):
                r = ROWS[t]
                v = v_b[0:r, t, :]
                link(dve.tensor_scalar(v, v, mv[0:r, t, 0:1], rstd[0:r, t:t + 1], ALU.subtract, ALU.mult))
                link(dve.tensor_tensor(v, v, gln_gb[0:r, 0, :], ALU.mult))
                dve.tensor_tensor(v, v, gln_gb[0:r, 1, :], ALU.add).then_inc(vg_ready, 1)
            for f in range(4):
                await_emptied(dve, ("g", f), 0)
                await_emptied(dve, ("g", f), 1)
                link(dve.tensor_scalar(merged[:, f, :], merged[:, f, :], gn_gla[:, f:f + 1], None, ALU.mult))
            await_full(dve, "ws")
            emptied(dve.tensor_tensor(wsT[:, :, :], bank("ws").rearrange("p (h n) -> p h n", h=H),
                                      upto[:, :].unsqueeze(1).to_broadcast([P, H, P]), ALU.mult), "ws")
            await_full(dve, "ws_s")
            emptied(dve.tensor_tensor(wsT_s[:, :, :], bank("ws_s")[0:NS, 0:H * NS].rearrange("p (h n) -> p h n", h=H),
                                      upto[0:NS, 0:NS].unsqueeze(1).to_broadcast([NS, H, NS]), ALU.mult), "ws_s")
            for c in range(NCH):
                await_full(dve, ("U", c))
                if c == 0:
                    emptied(dve.tensor_copy(S[:, 1, :, :], bank(("U", c))[:, 0:256].rearrange("p (r v) -> p r v", r=PAIRS)), ("U", c))
                    await_emptied(dve, ("U", c))
                    continue
                for p in range(PAIRS):
                    ins = dve.scalar_tensor_tensor(out=S[:, c + 1, p, :], in0=S[:, c, p, :], scalar=ebl[:, p, c:c + 1],
                                                   in1=bank(("U", c))[:, p * DV:(p + 1) * DV], op0=ALU.mult, op1=ALU.add)
                emptied(ins, ("U", c))
                await_emptied(dve, ("U", c))

            def rms(name, t):
                w = work[:, 2 if name == "ms" else 3, 0:4 * ROWS[t]]
                await_emptied(dve, (name, t))
                link(dve.reciprocal(w, w))
                return w.rearrange("p (h n) -> p h n", h=4)

            def causal_scores(t):
                r = ROWS[t]
                causal = (cum_p if t < NT - 1 else cum_s)[:, 1, :].bitcast(U32)
                if t == NT - 1:
                    link(dve.memset(scT[:, t % 2, :, 0:r], 0.0))
                for odd in range(2):
                    await_full(dve, ("sc", t), odd)
                    emptied(dve.copy_predicated(scT[0:r, t % 2, odd::2, 0:r], causal.unsqueeze(1).to_broadcast([r, 2, r]),
                                                heads(bank(("sc", t), odd)[0:r, :], r)[:, 0:2, :]), ("sc", t), odd)

            def gla_gated(t):
                for odd in range(2):
                    m = merged[:, odd:4:2, tok(t)]
                    dve.wait_ge(sq_gla, 2 * t + odd + 1)
                    emptied(dve.tensor_tensor(m, m, heads(bank(("o", t), odd), ROWS[t])[:, 0:2, :], ALU.mult), ("o", t), odd)

            def gla_normed(t):
                w = rms("ms", t)
                m = merged[:, 0:4, tok(t)]
                await_emptied(dve, ("o", t), 0)
                await_emptied(dve, ("o", t), 1)
                dve.tensor_tensor(m, m, w, ALU.mult).then_inc(gla_ready, 1)

            def gmlp_gated(t):
                m = merged[:, 4:8, tok(t)]
                if t == 0:
                    for f in range(4):
                        await_emptied(dve, ("u", f), 0)
                        await_emptied(dve, ("u", f), 1)
                r = ROWS[t]
                await_full(dve, ("sgu", t))
                gates, gated = work[:, 1, 0:H * r], bank(("sgu", t))[:, 0:H * r]
                if t < NT - 1:
                    ins = dve.tensor_tensor(gates.rearrange("p (h n) -> p h n", h=H), gated.rearrange("p (h n) -> p h n", h=H),
                                            bs[:, :, :], ALU.add)
                else:
                    ins = dve.tensor_tensor(gates.rearrange("p (h b s) -> p h b s", h=H, b=DB), gated.rearrange("p (h b s) -> p h b s", h=H, b=DB),
                                            bs[:, :, 0:DS].unsqueeze(2).to_broadcast([P, H, DB, DS]), ALU.add)
                emptied(ins, ("sgu", t))
                await_emptied(dve, ("sgu", t))
                dve.tensor_tensor(m, m, gates.rearrange("p (h n) -> p h n", h=H), ALU.mult).then_inc(u_gated, 1)

            def gmlp_normed(t):
                w = rms("mg", t)
                dve.wait_ge(u_gated, t + 1)
                for h in range(H):
                    ins = dve.scalar_tensor_tensor(out=merged[:, 4 + h, tok(t)], in0=merged[:, 4 + h, tok(t)], scalar=gn_gmlp[:, h:h + 1],
                                                   in1=w[:, h, :], op0=ALU.mult, op1=ALU.mult)
                ins.then_inc(gmlp_ready, 1)

            def norm_stats(t, ready):
                r = ROWS[t]
                if t:
                    dve.wait_ge(ready, t)
                for n in range(2):
                    link(dve.bn_stats(stats[0:r, n, :], x_sb[0:r, t, n * 512:(n + 1) * 512]))
                dve.bn_aggr(mv1[0:r, t, :], stats[0:r, :, :].rearrange("p a b -> p (a b)")).then_inc(ready, 1)

            def norm(t, std, ready):
                r = ROWS[t]
                x = x_sb[0:r, t, :]
                dve.wait_ge(std, t + 1)
                link(dve.reciprocal(rstd1[0:r, t:t + 1], rstd1[0:r, t:t + 1]))
                link(dve.tensor_scalar(x, x, mv1[0:r, t, 0:1], rstd1[0:r, t:t + 1], ALU.subtract, ALU.mult))
                link(dve.tensor_tensor(x, x, ln_gb[0:r, 0, :], ALU.mult))
                dve.tensor_tensor(x, x, ln_gb[0:r, 1, :], ALU.add).then_inc(ready, 1)

            def turned_half(t):
                await_full(dve, ("hT", t, 1))
                emptied(dve.tensor_copy(xT[:, 4:8, tok(t)], heads(bank(("hT", t, 1)), ROWS[t])), ("hT", t, 1))

            causal_scores(0)
            for t in range(NT - 1):
                gla_gated(t)
                causal_scores(t + 1)
                if t:
                    gla_normed(t - 1)
                if t == 3:
                    gmlp_normed(0)
                if t >= 2:
                    gmlp_gated(t - 2)
            gla_normed(3)
            gla_gated(4)
            gmlp_normed(1)
            gmlp_gated(2)
            gla_normed(4)
            for p in range(PAIRS):
                link(dve.tensor_tensor(S0[:, p, :, :], S0[:, p, :, :], ebl_s[:, p, :].unsqueeze(2).to_broadcast([P, DB, DV]), ALU.mult))
                for half in range(2):
                    await_full(dve, "Us", 2 * p + half)
                    ins = dve.tensor_tensor(S0[:, p, 4 * half:4 * half + 4, :], S0[:, p, 4 * half:4 * half + 4, :],
                                            bank("Us", 2 * p + half).rearrange("p (b v) -> p b v", b=4), ALU.add)
                    emptied(ins, "Us", 2 * p + half)
                    await_emptied(dve, "Us", 2 * p + half)
            for t in range(NT):
                r = ROWS[t]
                for n in range(2):
                    await_full(dve, ("m", t), n)
                    x = x_sb[0:r, t, n * 512:(n + 1) * 512]
                    rows = slice(0, P) if t < NT - 1 else slice(n * NS, (n + 1) * NS)
                    emptied(dve.scalar_tensor_tensor(out=x, in0=x, scalar=ALPHA, in1=bank(("m", t), n)[rows, :],
                                                     op0=ALU.mult, op1=ALU.add), ("m", t), n)
                if t < 3:
                    gmlp_normed(t + 2)
                if t < 2:
                    gmlp_gated(t + 3)
                if t:
                    turned_half(t - 1)
                await_emptied(dve, ("m", t), 0)
                await_emptied(dve, ("m", t), 1)
                norm_stats(t, var1_ready)
                norm(t, std1_ready, h_ready)
            turned_half(NT - 1)

            def all3(view):
                return view.rearrange("p (t e) -> p t e", t=NT)

            s, mask, sbias = scratch(0, NT * NE), scratch(1, NT * NE), scratch(3, NT * NE)
            t1, t2 = scratch(4, NT * NE), scratch(5, NT * NE)
            m1, m2, cnt2, gs = (scratch(6, 4 * NT * NG)[:, n * NT * NG:(n + 1) * NT * NG] for n in range(4))
            m8 = scratch(7, 8)
            sums = scratch(7, 8 + NT)[:, 8:8 + NT]
            last = slice((NT - 1) * NE, NT * NE)

            def by8(view):
                return view.rearrange("p (g e) -> p g e", e=GE)

            def over8(view):
                return view.unsqueeze(2).to_broadcast([P, NT * NG, GE])

            await_emptied(dve, ("logits", 0))
            link(dve.memset(s[NS:P, last], 0.0))
            for t in range(NT):
                await_emptied(dve, ("logits", t))
            link(dve.tensor_tensor(all3(sbias), all3(s), rbias[:, :].unsqueeze(1).to_broadcast([P, NT, NE]), ALU.add))
            link(dve.tensor_reduce(m1, by8(sbias), AX.X, ALU.max))
            link(dve.tensor_tensor(by8(t1), by8(sbias), over8(m1), ALU.is_equal))
            link(dve.tensor_reduce(cnt2, by8(t1), AX.X, ALU.add))
            link(dve.scalar_tensor_tensor(out=t1, in0=t1, scalar=NEG, in1=sbias, op0=ALU.mult, op1=ALU.add))
            link(dve.tensor_reduce(m2, by8(t1), AX.X, ALU.max))
            link(dve.tensor_scalar(cnt2, cnt2, 1.5, NEG, ALU.is_lt, ALU.mult))
            link(dve.tensor_tensor(cnt2, cnt2, m1, ALU.add))
            link(dve.tensor_tensor(m2, m2, cnt2, ALU.max))
            link(dve.tensor_tensor(gs, m1, m2, ALU.add))
            g4 = [NT, NG, NG]
            this = gs.rearrange("p (t g) -> p t g", t=NT).unsqueeze(3).to_broadcast([P] + g4)
            other = gs.rearrange("p (t g) -> p t g", t=NT).unsqueeze(2).to_broadcast([P] + g4)
            v1, v2 = (v.rearrange("p (t g o) -> p t g o", t=NT, g=NG) for v in (t1, t2))
            link(dve.tensor_tensor(v1, other, this, ALU.is_equal))
            link(dve.tensor_tensor(v1, v1, tri8[:, :, :].unsqueeze(1).to_broadcast([P] + g4), ALU.mult))
            link(dve.tensor_tensor(v2, other, this, ALU.is_gt))
            link(dve.tensor_tensor(t1, t1, t2, ALU.add))
            link(dve.tensor_reduce(m1, by8(t1), AX.X, ALU.add))
            link(dve.tensor_scalar(m1, m1, TOPG - 0.5, NEG, ALU.is_ge, ALU.mult))
            link(dve.tensor_tensor(by8(sbias), by8(sbias), over8(m1), ALU.add))
            for t in range(NT):
                c = slice(t * NE, (t + 1) * NE)
                link(dve.max(m8, sbias[:, c]))
                link(dve.match_replace(t1[:, c], m8, sbias[:, c], 4 * NEG))
            link(dve.tensor_tensor(mask, sbias, t1, ALU.not_equal))
            dve.memset(mask[NS:P, last], 0.0).then_inc(mask_ready, 1)
            dve.wait_ge(mask_ready, 1)
            link(dve.tensor_tensor(t2, s, mask, ALU.mult))
            link(dve.tensor_reduce(sums, all3(t2), AX.X, ALU.add))
            link(dve.memset(sums[NS:P, NT - 1:NT], 1.0))
            link(dve.reciprocal(sums, sums))
            link(dve.tensor_tensor(all3(t2), all3(t2), sums.unsqueeze(2).to_broadcast([P, NT, NE]), ALU.mult))
            link(dve.tensor_scalar(t2, t2, ROUTE_SCALE, None, ALU.mult))
            w = all3(t2)
            link(dve.tensor_copy(aux[:, :, 0:NE, 2], w))
            link(dve.tensor_tensor(w, w, aux[:, :, 0:NE, 2], ALU.subtract))
            link(dve.tensor_copy(aux[:, :, 0:NE, 3], w))
            link(dve.tensor_tensor(w, w, aux[:, :, 0:NE, 3], ALU.subtract))
            link(dve.tensor_copy(aux[:, :, 0:NE, 4], w))
            await_full(dve, "pos")
            emptied(dve.scalar_tensor_tensor(out=posm[:, :, 0:NE], in0=all3(mask), scalar=HIT, in1=all3(bank("pos")[:, 0:NT * NE]),
                                             op0=ALU.mult, op1=ALU.add), "pos")
            await_full(dve, "cnt")
            emptied(dve.tensor_reduce(m8[0:1, 0:1], bank("cnt")[0:1, 0:NE], AX.X, ALU.max), "cnt")
            await_emptied(dve, "cnt")
            dve.tensor_scalar(crowded[:, :], m8[0:1, 0:1], P + 0.5, None, ALU.is_gt).then_inc(route_ready, 1)

            base = count[0]

            class Chain:

                def __init__(self, start, j, per, of=dve_step):
                    self.start, self.j, self.per, self.n, self.sem = start, j, per, 0, of

                def __call__(self, ins):
                    self.n += 1
                    ins.then_inc(self.sem, 1)
                    dve.wait_ge(self.sem, self.start + self.j * self.per + self.n)

            def one_hot(u, e):
                dve.tensor_tensor(onehot[:, u, :, :], posm[:, :, bass.ds(e, 1)].to_broadcast([P, NT, P]),
                                  slot10k[:, :].unsqueeze(1).to_broadcast([P, NT, P]), ALU.is_equal).then_inc(onehot_ready, 1)

            def row_of_slots(u, keep, chain):
                chain(dve.tensor_tensor(metaf[:, 0:1], meta[:, 0:1], meta[:, 1:2], ALU.add))
                chain(dve.tensor_scalar(metaf[:, 1:2], metaf[:, 0:1], 0.0, part[:, 0:1], ALU.is_equal, ALU.mult))
                outs = (idx[:, u:u + 1],) if keep is None else (keep, idx[:, u:u + 1])
                for out in outs:
                    ins = dve.scalar_tensor_tensor(out=out, in0=metaf[:, 1:2], scalar=float(N), in1=metaf[:, 0:1], op0=ALU.add, op1=ALU.add)
                return ins

            def told(u, e, chain):
                dve.wait_ge(meta_full, e + 1)
                dve.tensor_copy(meta[:, :], psum[:, 7, 0:MC]).then_inc(meta_taken, 1)
                dve.wait_ge(meta_taken, e + 1)
                dve.scalar_tensor_tensor(out=wt_all[:, bass.ds(e, 1)], in0=meta[:, 2:3], scalar=meta[:, 3:4], in1=meta[:, 4:5],
                                         op0=ALU.add, op1=ALU.add)
                row_of_slots(u, row_all[:, bass.ds(e, 1)], chain).then_inc(idx_ready, 1)

            def rows_half(u, n):
                dve.wait_ge(T_full, n)
                dve.tensor_copy(hgT[:, u, 512:1024], psum[:, 3, :]).then_inc(TB_ready, 1)

            def hidden(u, n, e):
                dve.wait_ge(silu_ready, n)
                dve.scalar_tensor_tensor(out=hid[:, u, :], in0=sg[:, u, :], scalar=wt_all[:, bass.ds(e, 1)],
                                         in1=psum[:, u, FE:2 * FE], op0=ALU.mult, op1=ALU.mult).then_inc(hid_ready, 1)

            one_hot(0, 0)
            one_hot(1, 1)
            chain = Chain(count[0], 0, 0)
            told(0, 0, chain)
            one_hot(0, 2)
            told(1, 1, chain)
            one_hot(1, 3)
            rows_half(0, 2)
            told(0, 2, chain)
            one_hot(0, 4)
            rows_half(1, 4)
            told(1, 3, chain)
            hidden(0, 1, 0)
            base = count[0] + chain.n

            def expert_steps(u, j, chain):
                i = 2 * j + u
                left = NE - i if isinstance(j, int) else NE
                dve.wait_ge(hidT_full, i + 1)
                dve.tensor_copy(hidT[:, u, :], psum[:, 6, 0:FK * P]).then_inc(hidT_ready, 1)
                if left > AHEAD + 1:
                    one_hot(1 - u, i + AHEAD + 1)
                if left > 1:
                    hidden(1 - u, i + 2, i + 1)
                if left > 2:
                    rows_half(u, 2 * i + 6)
                if left > AHEAD:
                    told(u, i + AHEAD, chain)
                if not (isinstance(j, int) and j == 0):
                    dve.wait_ge(added, 16 * (i - 1))
                chain(dve.tensor_copy(yrow[:, u:u + 1], row_all[:, bass.ds(i, 1)]))
                dve.wait_ge(y_full, 2 * i + 2)
                dve.tensor_copy(y_sb[:, u, 512:1024], psum[:, 5, :]).then_inc(yB_ready, 1)

            chain = Chain(base, 0, 0)
            expert_steps(0, 0, chain)
            expert_steps(1, 0, chain)
            base += chain.n
            PER = chain.n
            with dve.Fori(1, NE // 2 - 3) as j:
                chain = Chain(base - PER, j, PER)
                expert_steps(0, j, chain)
                expert_steps(1, j, chain)
                assert chain.n == PER
            chain = Chain(base + (NE // 2 - 4) * PER, 0, 0)
            for j in range(NE // 2 - 3, NE // 2):
                expert_steps(0, j, chain)
                expert_steps(1, j, chain)
            count[0] = base + (NE // 2 - 4) * PER + chain.n

            class Further:

                def move(self, b):
                    dve.tensor_scalar(posm[:, :, 0:NE], posm[:, :, 0:NE], -float(P), None, ALU.add).then_inc(x_moved, 1)
                    dve.wait_ge(x_moved, b + 1)
                    dve.sem_inc(x_passed, 1)

                def __call__(self, e, n):
                    chain = Chain(0, n - 1, 4, x_step)
                    dve.tensor_tensor(onehot[:, 0, :, :], posm[:, :, bass.ds(e, 1)].to_broadcast([P, NT, P]),
                                      slot10k[:, :].unsqueeze(1).to_broadcast([P, NT, P]), ALU.is_equal).then_inc(x_onehot, 1)
                    dve.wait_ge(x_meta, n)
                    chain(dve.tensor_copy(meta[:, :], psum[:, 7, 0:MC]))
                    chain(dve.scalar_tensor_tensor(out=wt_all[:, 0:1], in0=meta[:, 2:3], scalar=meta[:, 3:4], in1=meta[:, 4:5],
                                                   op0=ALU.add, op1=ALU.add))
                    row_of_slots(0, None, chain).then_inc(x_idx, 1)
                    dve.wait_ge(x_silu, n)
                    dve.scalar_tensor_tensor(out=hid[:, 0, :], in0=sg[:, 0, :], scalar=wt_all[:, 0:1], in1=psum[:, 0, FE:2 * FE],
                                             op0=ALU.mult, op1=ALU.mult).then_inc(x_hid, 1)
                    dve.wait_ge(x_hidT_full, n)
                    dve.tensor_copy(hidT[:, 0, :], psum[:, 6, 0:FK * P]).then_inc(x_hidT, 1)

            further_slots(dve, Further(), lambda: dve.wait_ge(added, 16 * NE))

            def gain2(t):
                r = ROWS[t]
                x = x_sb[0:r, t, :]
                dve.wait_ge(normed2, t + 1)
                dve.tensor_tensor(x, x, ln_gb[0:r, 0, :], ALU.mult).then_inc(gained2, 1)
                if t >= NT - 2:
                    dve.wait_ge(gained2, t + 1)
                    dve.tensor_tensor(x, x, ln_gb[0:r, 1, :], ALU.add).then_inc(last_ready, 1)

            def scale2(t):
                r = ROWS[t]
                dve.wait_ge(std2_ready, t + 1)
                link(dve.reciprocal(rstd1[0:r, t:t + 1], rstd1[0:r, t:t + 1]))
                dve.scalar_tensor_tensor(out=mv1[0:r, t, 0:1], in0=mv1[0:r, t, 0:1], scalar=-1.0, in1=rstd1[0:r, t:t + 1],
                                         op0=ALU.mult, op1=ALU.mult).then_inc(scale2_ready, 1)

            dve.wait_ge(ln2_loaded, 32)
            for t in range(NT):
                dve.wait_ge(sum_loaded[t], 16)
                norm_stats(t, var2_ready)
                if t:
                    scale2(t - 1)
                if t > 1:
                    gain2(t - 2)
            scale2(NT - 1)
            gain2(NT - 2)
            gain2(NT - 1)


_INS = ["x_prompt", "x_sample", "state_gla", "w_in", "w_a_up", "b_a", "gla_norm_g", "gmlp_ln_g", "gmlp_ln_b",
        "w_s", "b_s", "gmlp_norm_g", "w_out", "ln1_g", "ln1_b", "w_router", "router_bias", "w_gate", "w_up",
        "w_down", "ws_gate", "ws_up", "ws_down", "ln2_g", "ln2_b"]
_OUTS = [(1, 512, 1024), (8, 8, 1024), (1, 1, 4, 64, 128), (1, 8, 4, 64, 128), (1, 8, 8, 512)]


def kernel(**inputs):
    import numpy as _np
    import concourse.bacc as _bacc
    from concourse.bass_utils import run_bass_kernel_spmd as _run

    nc = _bacc.Bacc("TRN2", target_bir_lowering=False, num_devices=1)
    arrays, args = {}, []
    for name in _INS:
        a = _np.ascontiguousarray(inputs[name])
        arrays[f"in_{name}_dram"] = a
        args.append(nc.dram_tensor(f"in_{name}_dram", a.shape, mybir.dt.from_np(a.dtype), kind="ExternalInput").ap())
    for i, shape in enumerate(_OUTS):
        args.append(nc.dram_tensor(f"out_{i}_dram", shape, F32, kind="ExternalOutput").ap())
    hybrid_layer(nc, *args)
    r = _run(nc, [arrays], core_ids=[0])
    return tuple(r.results[0][f"out_{i}_dram"] for i in range(len(_OUTS)))
```
